# Optimizing a Trainium2 kernel written in Bass

```python
import math
import jax, jax.numpy as jnp
from jax import lax
import numpy as np

D_MODEL = 2048
BATCH = 1
SEQ = 256
DEPTH = 1

CHUNK = 64
N_MIXERS = 2
EPS = 1e-6

GLA_HEADS = 4
GLA_KEY_WIDTH = D_MODEL // 2
GLA_VAL_WIDTH = D_MODEL
GLA_DK = GLA_KEY_WIDTH // GLA_HEADS
GLA_DV = GLA_VAL_WIDTH // GLA_HEADS
GLA_GATE_RANK = 16
GLA_GATE_TEMP = 16.0
GLA_IN_WIDTH = 2 * GLA_KEY_WIDTH + 2 * GLA_VAL_WIDTH + GLA_GATE_RANK

S5_WIDTH = D_MODEL // 2
S5_GROUP = 16
S5_GROUPS = S5_WIDTH // S5_GROUP
S5_STATE = 64
S5_DT_MIN = 1e-3
S5_DT_MAX = 1e-1
S5_EIG_CLIP = -1e-4

MLP_HIDDEN = 4 * D_MODEL


def _rmsnorm(x, g):
    xf = x.astype(jnp.float32)
    y = xf * lax.rsqrt(jnp.mean(xf * xf, axis=-1, keepdims=True) + EPS)
    return (y * g.astype(jnp.float32)).astype(x.dtype)

def _gla_mixer(h, w_in, w_gate_up, b_gate, o_norm, w_out):
    bsz, seq, _ = h.shape
    nc = seq // CHUNK
    proj = h @ w_in
    q, k, v, r, g_low = jnp.split(
        proj,
        [GLA_KEY_WIDTH, 2 * GLA_KEY_WIDTH, 2 * GLA_KEY_WIDTH + GLA_VAL_WIDTH,
         2 * GLA_KEY_WIDTH + 2 * GLA_VAL_WIDTH], axis=-1)
    log_a = jax.nn.log_sigmoid((g_low @ w_gate_up + b_gate).astype(jnp.float32)) / GLA_GATE_TEMP

    def to_chunks(t, dh):
        return t.reshape(bsz, nc, CHUNK, GLA_HEADS, dh).transpose(1, 0, 3, 2, 4).astype(jnp.float32)

    qc = to_chunks(q, GLA_DK) * (GLA_DK ** -0.5)
    kc = to_chunks(k, GLA_DK)
    vc = to_chunks(v, GLA_DV)
    ac = to_chunks(log_a, GLA_DK)
    cum = jnp.cumsum(ac, axis=3)
    total = cum[:, :, :, -1:, :]
    k_dec = kc * jnp.exp(total - cum)
    chunk_decay = jnp.exp(total[:, :, :, 0, :])

    def step(state, xs):
        q_c, k_c, v_c, d_c = xs
        state = d_c[..., None] * state + jnp.einsum('bhck,bhcv->bhkv', k_c, v_c)
        return state, jnp.einsum('bhck,bhkv->bhcv', q_c, state)

    s0 = jnp.zeros((bsz, GLA_HEADS, GLA_DK, GLA_DV), jnp.float32)
    _, o = lax.scan(step, s0, (qc, k_dec, vc, chunk_decay))
    o = o * lax.rsqrt(jnp.mean(o * o, axis=-1, keepdims=True) + EPS) * o_norm.astype(jnp.float32)
    o = o.transpose(1, 0, 3, 2, 4).reshape(bsz, seq, GLA_VAL_WIDTH).astype(h.dtype)
    return (o * jax.nn.silu(r)) @ w_out

def _s5_mixer(h, w_in, lam_re, lam_im, log_dt, b_re, b_im, c_re, c_im, d_skip, w_out):
    bsz, seq, _ = h.shape
    u = (h @ w_in).astype(jnp.float32)
    ug = u.reshape(bsz, seq, S5_GROUPS, S5_GROUP)
    lr = jnp.minimum(lam_re.astype(jnp.float32), S5_EIG_CLIP)
    li = lam_im.astype(jnp.float32)
    dt = jnp.exp(log_dt.astype(jnp.float32))[:, None]
    mag = jnp.exp(lr * dt)
    ang = li * dt
    ab_re = mag * jnp.cos(ang)
    ab_im = mag * jnp.sin(ang)
    den = lr * lr + li * li
    nr = ab_re - 1.0
    f_re = (nr * lr + ab_im * li) / den
    f_im = (ab_im * lr - nr * li) / den
    br = b_re.astype(jnp.float32)
    bi = b_im.astype(jnp.float32)
    bb_re = f_re[..., None] * br - f_im[..., None] * bi
    bb_im = f_re[..., None] * bi + f_im[..., None] * br
    bu_re = jnp.einsum('gnc,blgc->blgn', bb_re, ug)
    bu_im = jnp.einsum('gnc,blgc->blgn', bb_im, ug)
    a_re = jnp.broadcast_to(ab_re, bu_re.shape)
    a_im = jnp.broadcast_to(ab_im, bu_im.shape)

    def combine(e1, e2):
        a1r, a1i, b1r, b1i = e1
        a2r, a2i, b2r, b2i = e2
        return (a2r * a1r - a2i * a1i,
                a2r * a1i + a2i * a1r,
                a2r * b1r - a2i * b1i + b2r,
                a2r * b1i + a2i * b1r + b2i)

    _, _, x_re, x_im = lax.associative_scan(combine, (a_re, a_im, bu_re, bu_im), axis=1)
    y = (jnp.einsum('gcn,blgn->blgc', c_re.astype(jnp.float32), x_re)
         - jnp.einsum('gcn,blgn->blgc', c_im.astype(jnp.float32), x_im))
    y = y.reshape(bsz, seq, S5_WIDTH) + d_skip.astype(jnp.float32) * u
    y = jax.nn.gelu(y).astype(h.dtype)
    val, gate = jnp.split(y @ w_out, 2, axis=-1)
    return val * jax.nn.sigmoid(gate)

def _sq_relu_mlp(h, w_up, w_down):
    a = jax.nn.relu(h @ w_up)
    return (a * a) @ w_down

def first_inputs(seed: int = 0) -> dict:
    key = jax.random.key(seed)
    ks = jax.random.split(key, 24)
    n_gla = len(range(0, DEPTH, N_MIXERS))
    n_s5 = len(range(1, DEPTH, N_MIXERS))
    res_scale = (2 * DEPTH) ** -0.5

    def nrm(k, shape, scale):
        return jax.random.normal(k, shape, jnp.float32) * scale

    def gain(k, shape):
        return 1.0 + 0.02 * jax.random.normal(k, shape, jnp.float32)

    lam_im0 = math.pi * jnp.arange(S5_STATE, dtype=jnp.float32)
    return {
        'x': jax.random.normal(ks[0], (BATCH, SEQ, D_MODEL), jnp.float32),
        'gla_norm': gain(ks[1], (n_gla, D_MODEL)),
        'gla_w_in': nrm(ks[2], (n_gla, D_MODEL, GLA_IN_WIDTH), D_MODEL ** -0.5),
        'gla_w_gate_up': nrm(ks[3], (n_gla, GLA_GATE_RANK, GLA_KEY_WIDTH), GLA_GATE_RANK ** -0.5),
        'gla_b_gate': 1.0 + 0.1 * jax.random.normal(ks[4], (n_gla, GLA_KEY_WIDTH), jnp.float32),
        'gla_o_norm': gain(ks[5], (n_gla, GLA_DV)),
        'gla_w_out': nrm(ks[6], (n_gla, GLA_VAL_WIDTH, D_MODEL), GLA_VAL_WIDTH ** -0.5 * res_scale),
        's5_norm': gain(ks[7], (n_s5, D_MODEL)),
        's5_w_in': nrm(ks[8], (n_s5, D_MODEL, S5_WIDTH), D_MODEL ** -0.5),
        's5_lam_re': -0.5 + 0.01 * jax.random.normal(ks[9], (n_s5, S5_GROUPS, S5_STATE), jnp.float32),
        's5_lam_im': lam_im0 + 0.01 * jax.random.normal(ks[10], (n_s5, S5_GROUPS, S5_STATE), jnp.float32),
        's5_log_dt': jax.random.uniform(ks[11], (n_s5, S5_GROUPS), jnp.float32,
                                        minval=math.log(S5_DT_MIN), maxval=math.log(S5_DT_MAX)),
        's5_b_re': nrm(ks[12], (n_s5, S5_GROUPS, S5_STATE, S5_GROUP), (2 * S5_GROUP) ** -0.5),
        's5_b_im': nrm(ks[13], (n_s5, S5_GROUPS, S5_STATE, S5_GROUP), (2 * S5_GROUP) ** -0.5),
        's5_c_re': nrm(ks[14], (n_s5, S5_GROUPS, S5_GROUP, S5_STATE), (2 * S5_STATE) ** -0.5),
        's5_c_im': nrm(ks[15], (n_s5, S5_GROUPS, S5_GROUP, S5_STATE), (2 * S5_STATE) ** -0.5),
        's5_d': jax.random.normal(ks[16], (n_s5, S5_WIDTH), jnp.float32),
        's5_w_out': nrm(ks[17], (n_s5, S5_WIDTH, 2 * D_MODEL), S5_WIDTH ** -0.5 * res_scale),
        'mlp_norm': gain(ks[18], (DEPTH, D_MODEL)),
        'mlp_w_up': nrm(ks[19], (DEPTH, D_MODEL, MLP_HIDDEN), D_MODEL ** -0.5),
        'mlp_w_down': nrm(ks[20], (DEPTH, MLP_HIDDEN, D_MODEL), MLP_HIDDEN ** -0.5 * res_scale),
        'final_norm': gain(ks[21], (D_MODEL,)),
    }

def first_block(x, gla_norm, gla_w_in, gla_w_gate_up, gla_b_gate, gla_o_norm, gla_w_out,
              s5_norm, s5_w_in, s5_lam_re, s5_lam_im, s5_log_dt, s5_b_re, s5_b_im,
              s5_c_re, s5_c_im, s5_d, s5_w_out, mlp_norm, mlp_w_up, mlp_w_down, final_norm):
    h = x
    for i in range(DEPTH):
        j = i // N_MIXERS
        if i % N_MIXERS == 0:
            h = h + _gla_mixer(_rmsnorm(h, gla_norm[j]), gla_w_in[j], gla_w_gate_up[j],
                               gla_b_gate[j], gla_o_norm[j], gla_w_out[j])
        else:
            h = h + _s5_mixer(_rmsnorm(h, s5_norm[j]), s5_w_in[j], s5_lam_re[j], s5_lam_im[j],
                              s5_log_dt[j], s5_b_re[j], s5_b_im[j], s5_c_re[j], s5_c_im[j],
                              s5_d[j], s5_w_out[j])
        h = h + _sq_relu_mlp(_rmsnorm(h, mlp_norm[i]), mlp_w_up[i], mlp_w_down[i])
    return _rmsnorm(h, final_norm)


D_MIX = D_MODEL
SB_WIDTH = D_MIX // 2
LRU_WIDTH = D_MIX - SB_WIDTH
SB_HEAD_DIM = 128
SB_HEADS = SB_WIDTH // SB_HEAD_DIM
LRU_BLOCKS = 8
LRU_BLOCK_DIM = LRU_WIDTH // LRU_BLOCKS
CONV_WIDTH = 4
LRU_C = 8.0
Q_BLOCK = 128
D_IN = 4 * SB_WIDTH + 2 * LRU_WIDTH


def rmsnorm(x, gain):
    xf = x.astype(jnp.float32)
    y = xf * lax.rsqrt(jnp.mean(xf * xf, axis=-1, keepdims=True) + EPS)
    return (y * gain.astype(jnp.float32)).astype(x.dtype)

def stick_breaking_attention(q, k, v):
    B, H, S, Dh = q.shape
    n_blk = S // Q_BLOCK
    q_blocks = q.reshape(B, H, n_blk, Q_BLOCK, Dh).transpose(2, 0, 1, 3, 4)
    k_pos = jnp.arange(S, dtype=jnp.int32)
    scale = Dh ** -0.5

    def one_block(args):
        q_blk, blk = args
        z = jnp.einsum('bhqd,bhkd->bhqk', q_blk, k).astype(jnp.float32) * scale
        q_pos = blk * Q_BLOCK + jnp.arange(Q_BLOCK, dtype=jnp.int32)
        mask = k_pos[None, :] < q_pos[:, None]
        log_fail = jnp.where(mask, jax.nn.log_sigmoid(-z), 0.0)
        after = lax.cumsum(log_fail, axis=3, reverse=True) - log_fail
        log_w = jax.nn.log_sigmoid(z) + after
        w = jnp.where(mask, jnp.exp(log_w), 0.0)
        return jnp.einsum('bhqk,bhkd->bhqd', w.astype(v.dtype), v)

    out = lax.map(one_block, (q_blocks, jnp.arange(n_blk, dtype=jnp.int32)))
    return out.transpose(1, 2, 0, 3, 4).reshape(B, H, S, Dh)

def causal_depthwise_conv(x, w, b):
    S = x.shape[1]
    xp = jnp.pad(x, ((0, 0), (CONV_WIDTH - 1, 0), (0, 0)))
    out = xp[:, 0:S, :] * w[0]
    for i in range(1, CONV_WIDTH):
        out = out + xp[:, i:i + S, :] * w[i]
    return out + b

def rg_lru(x, w_a, b_a, w_x, b_x, lam):
    B, S, C = x.shape
    xb = x.reshape(B, S, LRU_BLOCKS, LRU_BLOCK_DIM)
    r = jax.nn.sigmoid(jnp.einsum('bsgi,gij->bsgj', xb, w_a).reshape(B, S, C) + b_a)
    i = jax.nn.sigmoid(jnp.einsum('bsgi,gij->bsgj', xb, w_x).reshape(B, S, C) + b_x)
    log_a = -LRU_C * r.astype(jnp.float32) * jax.nn.softplus(-lam.astype(jnp.float32))
    a = jnp.exp(log_a)
    u = jnp.sqrt(-jnp.expm1(2.0 * log_a)) * (i * x).astype(jnp.float32)

    def combine(left, right):
        a_l, b_l = left
        a_r, b_r = right
        return a_l * a_r, a_r * b_l + b_r

    _, h = lax.associative_scan(combine, (a, u), axis=1)
    return h.astype(x.dtype)

def second_inputs(seed: int = 0) -> dict:
    key = jax.random.key(seed)
    ks = jax.random.split(key, 14)
    L = DEPTH
    x = jax.random.normal(ks[0], (BATCH, SEQ, D_MODEL), jnp.float32)
    norm_gain = 1.0 + 0.02 * jax.random.normal(ks[1], (L, D_MODEL), jnp.float32)
    w_in = jax.random.normal(ks[2], (L, D_MODEL, D_IN), jnp.float32) * D_MODEL ** -0.5
    q_norm_gain = 1.0 + 0.02 * jax.random.normal(ks[3], (L, SB_HEAD_DIM), jnp.float32)
    k_norm_gain = 1.0 + 0.02 * jax.random.normal(ks[4], (L, SB_HEAD_DIM), jnp.float32)
    conv_w = jax.random.normal(ks[5], (L, CONV_WIDTH, LRU_WIDTH), jnp.float32) * CONV_WIDTH ** -0.5
    conv_b = 0.01 * jax.random.normal(ks[6], (L, LRU_WIDTH), jnp.float32)
    lru_w_a = jax.random.normal(ks[7], (L, LRU_BLOCKS, LRU_BLOCK_DIM, LRU_BLOCK_DIM), jnp.float32) * LRU_BLOCK_DIM ** -0.5
    lru_b_a = 0.01 * jax.random.normal(ks[8], (L, LRU_WIDTH), jnp.float32)
    lru_w_x = jax.random.normal(ks[9], (L, LRU_BLOCKS, LRU_BLOCK_DIM, LRU_BLOCK_DIM), jnp.float32) * LRU_BLOCK_DIM ** -0.5
    lru_b_x = 0.01 * jax.random.normal(ks[10], (L, LRU_WIDTH), jnp.float32)
    u = jax.random.uniform(ks[11], (L, LRU_WIDTH), jnp.float32, minval=0.9, maxval=0.999)
    s = u ** (1.0 / LRU_C)
    lru_lambda = jnp.log(s) - jnp.log1p(-s)
    w_out = jax.random.normal(ks[12], (L, D_MIX, D_MODEL), jnp.float32) * D_MIX ** -0.5
    return {"x": x, "norm_gain": norm_gain, "w_in": w_in, "q_norm_gain": q_norm_gain,
            "k_norm_gain": k_norm_gain, "conv_w": conv_w, "conv_b": conv_b,
            "lru_w_a": lru_w_a, "lru_b_a": lru_b_a, "lru_w_x": lru_w_x, "lru_b_x": lru_b_x,
            "lru_lambda": lru_lambda, "w_out": w_out}

def second_block(x, norm_gain, w_in, q_norm_gain, k_norm_gain, conv_w, conv_b,
              lru_w_a, lru_b_a, lru_w_x, lru_b_x, lru_lambda, w_out):
    B, S, _ = x.shape
    h = x
    for l in range(DEPTH):
        xn = rmsnorm(h, norm_gain[l])
        proj = jnp.einsum('bsd,de->bse', xn, w_in[l])
        q, k, v, g_sb, x_lru, g_lru = jnp.split(
            proj, np.cumsum([SB_WIDTH] * 4 + [LRU_WIDTH]).tolist(), axis=-1)

        def heads(t):
            return t.reshape(B, S, SB_HEADS, SB_HEAD_DIM)
        qh = rmsnorm(heads(q), q_norm_gain[l]).transpose(0, 2, 1, 3)
        kh = rmsnorm(heads(k), k_norm_gain[l]).transpose(0, 2, 1, 3)
        vh = heads(v).transpose(0, 2, 1, 3)
        y_sb = stick_breaking_attention(qh, kh, vh).transpose(0, 2, 1, 3).reshape(B, S, SB_WIDTH)
        y_sb = y_sb * jax.nn.silu(g_sb)

        xc = causal_depthwise_conv(x_lru, conv_w[l], conv_b[l])
        y_lru = rg_lru(xc, lru_w_a[l], lru_b_a[l], lru_w_x[l], lru_b_x[l], lru_lambda[l])
        y_lru = y_lru * jax.nn.silu(g_lru)

        y = jnp.concatenate([y_sb, y_lru], axis=-1)
        h = h + jnp.einsum('bse,ed->bsd', y, w_out[l])
    return h


def setup_inputs(seed=0):
    out = dict(first_inputs(seed))
    for name, value in second_inputs(seed + 1).items():
        if name != "x":
            out[name + "_2"] = value
    return out


def reference(
    x, gla_norm, gla_w_in, gla_w_gate_up, gla_b_gate, gla_o_norm, gla_w_out, s5_norm, s5_w_in,
    s5_lam_re, s5_lam_im, s5_log_dt, s5_b_re, s5_b_im, s5_c_re, s5_c_im, s5_d, s5_w_out,
    mlp_norm, mlp_w_up, mlp_w_down, final_norm, norm_gain_2, w_in_2, q_norm_gain_2,
    k_norm_gain_2, conv_w_2, conv_b_2, lru_w_a_2, lru_b_a_2, lru_w_x_2, lru_b_x_2, lru_lambda_2,
    w_out_2,
):
    x = first_block(
        x, gla_norm, gla_w_in, gla_w_gate_up, gla_b_gate, gla_o_norm, gla_w_out, s5_norm,
        s5_w_in, s5_lam_re, s5_lam_im, s5_log_dt, s5_b_re, s5_b_im, s5_c_re, s5_c_im, s5_d,
        s5_w_out, mlp_norm, mlp_w_up, mlp_w_down, final_norm,
    )
    return second_block(
        x, norm_gain_2, w_in_2, q_norm_gain_2, k_norm_gain_2, conv_w_2, conv_b_2, lru_w_a_2,
        lru_b_a_2, lru_w_x_2, lru_b_x_2, lru_lambda_2, w_out_2,
    )


_drawn_inputs = setup_inputs


def setup_inputs(seed=0):
    import zlib

    import numpy as np

    out = dict(_drawn_inputs(seed))
    spreads = {}
    factors = {'gla_norm': 3.004,
     'gla_o_norm': 6.191,
     'mlp_norm': 3.675,
     'norm_gain_2': 3.952,
     'q_norm_gain_2': 8.0,
     'k_norm_gain_2': 8.0,
     'conv_b_2': 4.145,
     'lru_b_a_2': 64.0,
     'lru_b_x_2': 40.338}
    for name, (base, spread) in spreads.items():
        noise = np.random.default_rng([zlib.crc32(name.encode()), seed]).standard_normal(out[name].shape)
        drawn = base * np.exp(spread * noise) if base else spread * noise
        out[name] = __import__('jax').numpy.asarray(drawn.astype(out[name].dtype))
    for name, factor in factors.items():
        out[name] = (out[name] * factor).astype(out[name].dtype)
    return out
```

```python
import concourse.bass as bass
from concourse import mybir
from contextlib import ExitStack

F32 = mybir.dt.float32
F32R = mybir.dt.float32r
ALU = mybir.AluOpType
ACT = mybir.ActivationFunctionType
AX = mybir.AxisListType

P = 128
D = 2048
S = 256
TT = S // P
KT = D // P
N = 512
CK = 2
CH = KT // CK
RING = 4
EPS = 1e-6
CHUNK = 64
GH = 4
GDK = 256
RANK = 16
HD = 128
SH = 8
LRU_C = 8.0
CONV = 4
MLP_BLOCKS = 4

KINDS = "kkqq" + "vr" * GH + "oooo" + ("uuuu" + "dddd") * (MLP_BLOCKS - 1) + "uuuuDDDD" \
    + "xxKKQQVVggll" + "ffff"
PANELS = len(KINDS)
FIRST_O = KINDS.index("o")
FIRST_U = KINDS.index("u")
FIRST_DL = KINDS.index("D")
FIRST_X = KINDS.index("x")
FIRST_F = KINDS.index("f")
BODY = 8

ST_X, ST_O, ST_MLP, ST_FIN, ST_N2, ST_KQ, ST_ALL = 0, 1, 5, 6, 7, 8, 12
ST_WIDTH = [TT] * ST_KQ + [TT * 4] * (ST_ALL - ST_KQ)


def count(kinds, p):
    return sum(k in kinds for k in KINDS[:p + 1])


def groups_before(turn):
    turned = sum(KINDS[q] in "qrouDxKQgl" for q in range(min(turn - 1, PANELS)))
    return CH + (4 if turn > 2 else 0) + 2 * turned


def at(f, t, it):
    v = f(t)
    if it is None:
        return v
    step = f(t + BODY) - v
    assert f(t + 2 * BODY) - f(t + BODY) == step
    return it * step + v if step else v


def gated_block_kernel(nc, x, gla_norm, gla_w_in, gla_w_gate_up, gla_b_gate, gla_o_norm, gla_w_out,
                       mlp_norm, mlp_w_up, mlp_w_down, final_norm, norm_gain_2, w_in_2,
                       q_norm_gain_2, k_norm_gain_2, conv_w_2, conv_b_2, lru_w_a_2, lru_b_a_2,
                       lru_w_x_2, lru_b_x_2, lru_lambda_2, w_out_2, out):
    ctx = ExitStack()
    with ctx:
        def sb(name, shape, dt=F32):
            return ctx.enter_context(nc.sbuf_tensor(name, shape, dt))

        def sem(name):
            return ctx.enter_context(nc.semaphore(name))

        raw = sb("raw", [P, RING, CK, N])
        w_hi = sb("w_hi", [P, RING, CK, N], F32R)
        w_lo = sb("w_lo", [P, RING, CK, N], F32R)
        xa_hi = sb("xa_hi", [P, KT, S], F32R)
        xa_lo = sb("xa_lo", [P, KT, S], F32R)
        xb_hi = sb("xb_hi", [P, KT, S], F32R)
        xb_lo = sb("xb_lo", [P, KT, S], F32R)
        h = sb("h", [P, TT, D])
        stage = sb("stage", [P, 2, TT, N])
        ident = sb("ident", [P, P])
        suffix = sb("suffix", [P, P])
        below = sb("below", [P, P])
        neg_ones = sb("neg_ones", [P, P])
        neg_mask = sb("neg_mask", [P, P])
        spans = sb("spans", [P, TT, 10])
        neg_half = sb("neg_half", [P, 8])
        rows = sb("rows", [P, P])
        par = sb("par", [P, P])
        qk_gain = sb("qk_gain", [P, 4])
        o_gain = sb("o_gain", [P, N])
        sums = sb("sums", [P, 80])
        ms = sb("ms", [P, ST_ALL, 8])
        rs = sb("rs", [P, ST_ALL, 8])
        scl = sb("scl", [P, 20])
        lru_par = sb("lru_par", [P, 40])
        ARENA = 16384
        arena_at = (nc.sbuf_usable_end - 4 * ARENA) // 64 * 64
        arena = nc.alloc_sbuf_tensor_at("arena", [P, ARENA], F32, offset=arena_at)
        gate_w = nc.alloc_sbuf_tensor_at("gate_w", [P, KT, P], F32R,
                                         offset=arena_at + 4 * (ARENA - KT * P))
        assert nc.sbuf_base <= arena_at

        def room(start, *dims):
            size = 1
            for n in dims:
                size *= n
            v = arena[:, start:start + size]
            if len(dims) == 2:
                v = v.rearrange("p (a b) -> p a b", b=dims[1])
            if len(dims) == 3:
                v = v.rearrange("p (a b c) -> p a b c", b=dims[1], c=dims[2])
            return v

        log_a = room(0, TT, 1024)
        z_gate = room(2048, 4, N)
        b_gate = room(4096, 1024)
        w_up_gate = room(5120, 1024)
        g_low = room(6144, S)
        wg_raw = room(6400, KT, RANK)
        scaled_q = room(0, 2, 2 * 10 * CHUNK)
        scores = room(2560, GH, 384)
        zt = room(4096, TT, N)
        keys = room(6656, TT, 1024)
        vals = room(6656, TT, N)
        th = room(7680, TT, N)
        key_t = room(8704, 8, S)
        qry_t = room(10752, 8, S)
        decay = room(12800, 8, 10)
        junk = room(8704, D)
        junk_o = room(12900, N)
        fin_gain = room(8192, D)
        junk_h = room(10240, N)
        lru_w = room(0, 2, 8, P)
        v2 = room(0, TT, 1024)
        q2_t = room(2048, 8, S)
        k2_t = room(4096, 8, S)
        lru_h = room(6144, 8, S)
        PAD = CONV - 1
        lru_x = room(8192, 4, PAD + S)
        conv = room(9228, 4, S)
        th_r = room(10252, 4, S)
        th_i = room(11276, 4, S)
        lru_a = room(12300, 4, S)
        lru_u = room(13324, 4, S)
        y_t = room(8192, 8, S)
        soft = room(10240, 2, 384)
        soft_sp = room(11008, 2, 384)
        wts = room(11776, 2, 384)
        zt2 = room(12544, TT, N)
        prod = room(13568, 2, N)
        sq2 = room(14592, TT, N)

        acc = ctx.enter_context(nc.psum_tensor("acc", [P, 2, TT, N], F32))
        tp = ctx.enter_context(nc.psum_tensor("tp", [P, 2, N], F32))
        aux = ctx.enter_context(nc.psum_tensor("aux", [P, 2, N], F32))

        raw_in = [sem(f"raw_in{i}") for i in range(RING)]
        hi_ready, lo_ready = sem("hi_ready"), sem("lo_ready")
        chunk_used = sem("chunk_used")
        acc_read_act, acc_read_dve = sem("acc_read_act"), sem("acc_read_dve")
        stage_act, stage_dve = sem("stage_act"), sem("stage_dve")
        tp_ready = sem("tp_ready")
        tp_hi, tp_lo = sem("tp_hi"), sem("tp_lo")
        norm_in = sem("norm_in")
        par_in, par_turned, par_ready = sem("par_in"), sem("par_turned"), sem("par_ready")
        x_in = [sem(f"x_in{i}") for i in range(4)]
        gain_in, up_in, wg_in = sem("gain_in"), sem("up_in"), sem("wg_in")
        consts, pool_chain = sem("consts"), sem("pool_chain")
        ms_ready, rs_ready = sem("ms_ready"), sem("rs_ready")
        sq_ready = sem("sq_ready")
        act_chain, dve_chain = sem("act_chain"), sem("dve_chain")
        wg_hi, wg_lo = sem("wg_hi"), sem("wg_lo")
        low_ready, low_out = sem("low_ready"), sem("low_out")
        gate_ready, gate_out = sem("gate_ready"), sem("gate_out")
        ln_ready, log_ready = sem("ln_ready"), sem("log_ready")
        span_ready, decay_ready = sem("span_ready"), sem("decay_ready")
        suf_ready, suf_out = sem("suf_ready"), sem("suf_out")
        keys_act, keys_ready = sem("keys_act"), sem("keys_ready")
        r1_ready = sem("r1_ready")
        sq_q, sc_ready, sc_act, sc_dve = sem("sq_q"), sem("sc_ready"), sem("sc_act"), sem("sc_dve")
        vals_act, vals_dve = sem("vals_act"), sem("vals_dve")
        o_ready, o_read = sem("o_ready"), sem("o_read")
        silu_act = sem("silu_act")
        h_added = sem("h_added")
        h_squared = sem("h_squared")
        relu_dve = sem("relu_dve")
        late_in = sem("late_in")
        r2_ready = sem("r2_ready")
        lam_act, lam_ready = sem("lam_act"), sem("lam_ready")
        conv_ready = sem("conv_ready")
        lru_mm, lru_th = sem("lru_mm"), sem("lru_th")
        lru_exp, lru_sq, lru_root, lru_done = sem("lru_exp"), sem("lru_sq"), sem("lru_root"), sem("lru_done")
        kq_sq, kq_red = sem("kq_sq"), sem("kq_red")
        v2_act, v2_dve = sem("v2_act"), sem("v2_dve")
        z_ready, ln_out, sp_out = sem("z_ready"), sem("ln_out"), sem("sp_out")
        lw_ready, w_out_s, y_ready, y_out = sem("lw_ready"), sem("w_out_s"), sem("y_ready"), sem("y_out")
        prod_out = sem("prod_out")
        out_ready = sem("out_ready")
        out_sent = [sem(f"out_sent{i}") for i in range(2)]

        def tiles(w):
            return w.rearrange("(k p) n -> p k n", p=P)

        w_in_v, w_out_v = tiles(gla_w_in[0]), tiles(gla_w_out[0])
        up_v, down_v = tiles(mlp_w_up[0]), tiles(mlp_w_down[0])
        in2_v, out2_v = tiles(w_in_2[0]), tiles(w_out_2[0])
        x_v = x[0].rearrange("(t p) d -> p t d", p=P)
        out_v = out[0].rearrange("(t p) d -> p t d", p=P)

        par_src = [(mlp_norm[0], 16), (final_norm, 16), (norm_gain_2[0], 16),
                   (conv_w_2[0], 32), (lru_lambda_2[0], 8), (lru_b_a_2[0], 8), (lru_b_x_2[0], 8),
                   (conv_b_2[0], 8)]
        C_GLA, C_MLP, C_N2, C_CONV, C_LAM, C_BA, C_BX, C_CB = 0, 16, 48, 64, 96, 104, 112, 120
        R1S, R1H, R2, R2H, RF2, T0, T1 = 0, 2, 4, 6, 8, 10, 12
        Q_X, Q_O, Q_M, Q_F, Q_N, Q_KQ = 0, 2, 10, 18, 26, 40
        L_SP, L_NEG, L_BA, L_BX, L_T = 0, 8, 16, 24, 32

        block = ctx.enter_context(nc.Block())

        @block.sync
        def _(sp):
            def load(c, n0, it, per, src):
                n = n0 + c
                if it is None:
                    if n >= RING:
                        sp.wait_ge(lo_ready, n - RING + 1)
                elif n >= RING:
                    sp.wait_ge(lo_ready, it * per + (n - RING + 1))
                sp.dma_start(raw[:, n % RING, :, :], src).then_inc(raw_in[n % RING], 16)

            def panel(n0, it, per, view, row, col):
                for c in range(CH):
                    load(c, n0, it, per, view[:, bass.ds(row + CK * c, CK), bass.ds(col, N)])

            sp.dma_start(rows[0:KT, :], gla_norm[0].rearrange("(b p) -> b p", p=P)).then_inc(norm_in, 16)
            panel(0, None, CH, w_in_v, 0, GH * GDK)
            panel(CH, None, CH, w_in_v, 0, GH * GDK + N)
            n = 2 * CH
            with sp.Fori(0, 2) as j:
                panel(n, j, CH, w_in_v, 0, j * N)
            n += 2 * CH
            with sp.Fori(0, GH) as j:
                panel(n, j, 2 * CH, w_in_v, 0, j * N + 2 * GH * GDK)
                panel(n + CH, j, 2 * CH, w_in_v, 0, j * N + 2 * GH * GDK + D)
            n += 2 * GH * CH
            with sp.Fori(0, 4) as j:
                panel(n, j, CH, w_out_v, 0, j * N)
            n += 4 * CH
            for b in range(MLP_BLOCKS):
                with sp.Fori(0, 4) as j:
                    panel(n, j, CH, up_v, 0, j * N + b * D)
                n += 4 * CH
                with sp.Fori(0, 4) as j:
                    panel(n, j, CH, down_v, b * KT, j * N)
                n += 4 * CH
            for first in (4096, 1024, 0, 2048, 3072, 5120):
                with sp.Fori(0, 2) as j:
                    panel(n, j, CH, in2_v, 0, j * N + first)
                n += 2 * CH
            with sp.Fori(0, 4) as j:
                panel(n, j, CH, out2_v, 0, j * N)
            for j in range(4):
                for tt in range(TT):
                    sp.wait_ge(out_ready, TT * j + tt + 1)
                    sp.dma_start(out_v[:, tt, j * N:(j + 1) * N], stage[:, j % 2, tt, :])\
                        .then_inc(out_sent[j % 2], 16)
            for s in out_sent:
                sp.wait_ge(s, 16 * TT * 2)

        @block.gpsimd
        def _(pool):
            steps = [0]

            def link(ins):
                steps[0] += 1
                ins.then_inc(pool_chain, 1)
                pool.wait_ge(pool_chain, steps[0])

            def triangle(m, value, op, base=0):
                link(pool.memset(m, value))
                link(pool.affine_select(out=m, in_=m, compare_op=op, fill=0.0, base=base,
                                        pattern=[[-1, P]], channel_multiplier=1))

            link(pool.memset(ident[:, :], 0.0))
            link(pool.affine_select(out=ident[:, :], in_=ident[:, :], compare_op=ALU.not_equal,
                                    fill=1.0, base=0, pattern=[[-1, P]], channel_multiplier=1))
            row = KT
            for src, k in par_src:
                if k == 32:
                    src = src.rearrange("w (b p) -> (w b) p", p=P)
                else:
                    src = src.rearrange("(b p) -> b p", p=P)
                pool.dma_start(rows[row:row + k, :], src).then_inc(par_in, 16)
                row += k
            pool.memset(neg_half[:, :], -0.5).then_inc(consts, 1)
            link(pool.memset(gate_w[:, :, :].bitcast(F32), 0.0))
            link(pool.memset(w_up_gate, 0.0))
            pool.dma_start(w_up_gate[0:RANK, :], gla_w_gate_up[0]).then_inc(up_in, 16)
            pool.dma_start(w_up_gate[32:32 + RANK, :], gla_w_gate_up[0]).then_inc(up_in, 16)
            pool.dma_start(b_gate, gla_b_gate[0].partition_broadcast(P)).then_inc(up_in, 16)
            pool.memset(spans[:, :, :], 0.0).then_inc(consts, 1)
            triangle(suffix[:, :], 1.0 / 16, ALU.is_gt)
            link(pool.affine_select(out=suffix[:, 0:CHUNK], in_=suffix[:, 0:CHUNK],
                                    compare_op=ALU.is_ge, fill=0.0, base=CHUNK - 1,
                                    pattern=[[0, CHUNK]], channel_multiplier=-1))
            for t, p0, a, b in ((0, 64, 1, 4), (1, 0, 2, 4), (1, 0, 5, 7), (1, 64, 3, 4),
                                (1, 64, 6, 7), (1, 64, 8, 9)):
                link(pool.memset(spans[p0:p0 + 64, t, a:b], 1.0 / 16))
            triangle(below[:, :], -1.0, ALU.is_ge)
            triangle(neg_mask[:, :], -2.0 ** 100, ALU.is_ge)
            pool.memset(neg_ones[:, :], -1.0).then_inc(consts, 1)
            pool.dma_start(qk_gain[:, 0:1], q_norm_gain_2[0].rearrange("(p a) -> p a", a=1)).then_inc(gain_in, 16)
            pool.dma_start(qk_gain[:, 1:2], k_norm_gain_2[0].rearrange("(p a) -> p a", a=1)).then_inc(gain_in, 16)
            pool.dma_start(o_gain[:, :], gla_o_norm[0].partition_broadcast(P)).then_inc(gain_in, 16)

            def power(i):
                pool.wait_ge(ms_ready, i + 1)
                w = ST_WIDTH[i]
                pool.tensor_tensor(rs[:, i, 0:w], ms[:, i, 0:w], neg_half[:, 0:w], ALU.pow)\
                    .then_inc(rs_ready, 1)

            pool.wait_ge(consts, 3)
            for i in range(ST_MLP):
                power(i)
            pool.wait_ge(chunk_used, CH * (FIRST_O + 1))
            pool.wait_ge(tp_lo, groups_before(FIRST_O + 1))
            pool.dma_start(fin_gain, final_norm.partition_broadcast(P)).then_inc(late_in, 16)
            pool.dma_start(lru_w[:, 0, :, :], lru_w_a_2[0].rearrange("g i j -> i g j")).then_inc(late_in, 16)
            pool.dma_start(lru_w[:, 1, :, :], lru_w_x_2[0].rearrange("g i j -> i g j")).then_inc(late_in, 16)
            for i in range(ST_MLP, ST_ALL):
                power(i)

        @block.tensor
        def _(pe):
            def operand(kind):
                return (xa_hi, xa_lo) if kind in "kqvruxKQVgl" else (xb_hi, xb_lo)

            def multiply(t, c, it):
                n = CH * t + c
                xh, xl = operand(KINDS[t])
                if c == 0:
                    if t >= 2:
                        for s, kinds in ((acc_read_act, "kqvruxKQVgl"), (acc_read_dve, "kqvouDdxKQVf")):
                            pe.wait_ge(s, at(lambda q: count(kinds, q - 2), t, it))
                first = KINDS[t] != KINDS[t - 1] and KINDS[t] in "oudDxf" or t == 0
                if first:
                    if t == 0:
                        pe.wait_ge(tp_lo, c + 1)
                    else:
                        src = {"o": lambda q: FIRST_O - 8 + 1 + 2 * (c // 2),
                               "u": lambda q: (q if q == FIRST_U else FIRST_U) - 4 + c // 2,
                               "d": lambda q: q - 4 + c // 2, "D": lambda q: q - 4 + c // 2,
                               "x": lambda q: q - 4 + c // 2, "f": lambda q: q - 4 + c // 2}[KINDS[t]]
                        pe.wait_ge(tp_lo, at(lambda q: groups_before(src(q) + 1) + c % 2 + 1, t, it))
                pe.wait_ge(lo_ready, at(lambda q: CH * q + c + 1, t, it))
                for k in range(CK):
                    kt = CK * c + k
                    for tt in range(TT):
                        o = acc[:, t % 2, tt, :]
                        xs = slice(tt * P, (tt + 1) * P)
                        pe.matmul(o, xh[:, kt, xs], w_hi[:, n % RING, k, :], start=kt == 0, stop=False)
                        pe.matmul(o, xh[:, kt, xs], w_lo[:, n % RING, k, :], start=False, stop=False)
                        last = pe.matmul(o, xl[:, kt, xs], w_hi[:, n % RING, k, :], start=False,
                                         stop=kt == KT - 1)
                last.then_inc(chunk_used, 1)

            def group(g0, g, it_wait, src):
                if it_wait is not None:
                    pe.wait_ge(tp_hi, it_wait)
                    pe.wait_ge(tp_lo, it_wait)
                for k in range(2):
                    for tt in range(TT):
                        last = pe.transpose(tp[:, g % 2, (2 * k + tt) * P:(2 * k + tt + 1) * P],
                                            src(k, tt), ident[:, :])
                last.then_inc(tp_ready, 1)

            def turn_panel(t, it):
                q = t - 1
                kind = KINDS[q]
                if kind in "qx":
                    pe.wait_ge(stage_act, at(lambda u: count("quxKQ", u - 1), t, it))
                if kind == "o":
                    pe.wait_ge(h_added, count("odD", q))
                else:
                    pe.wait_ge(stage_dve, at(lambda u: count("qruDxKQgl", u - 1), t, it))
                for g in range(2):
                    def src(k, tt):
                        f = 2 * g + k
                        if kind in "oD":
                            j = (q - KINDS.index(kind)) * 4 + f
                            return h[:, tt, j * P:(j + 1) * P]
                        return stage[:, q % 2, tt, f * P:(f + 1) * P]
                    group(None, g, at(lambda u: groups_before(u) + g - 1, t, it), src)

            def turn_x(g):
                if g % 2 == 0:
                    pe.wait_ge(x_in[g // 2], 16)
                group(0, g, g - 1 if g >= 2 else None,
                      lambda k, tt: h[:, tt, (2 * g + k) * P:(2 * g + k + 1) * P])

            def gate_low():
                pe.wait_ge(wg_lo, 1)
                pe.wait_ge(tp_lo, CH)
                for kt in range(KT):
                    for i, xs in enumerate((xa_hi, xa_lo)):
                        last = pe.matmul(aux[:, 0, 0:S], gate_w[:, kt, :], xs[:, kt, :],
                                         start=kt == 0 and i == 0, stop=kt == KT - 1 and i == 1)
                last.then_inc(low_ready, 1)

            def gate_up(i):
                tt, half = divmod(i, 2)
                pe.wait_ge(low_out, 1)
                if i >= 2:
                    pe.wait_ge(gate_out, i - 1)
                else:
                    pe.wait_ge(up_in, 48)
                pe.matmul(aux[:, (i + 1) % 2, :], g_low[:, tt * P:(tt + 1) * P],
                          w_up_gate[:, half * N:(half + 1) * N], start=True, stop=True)\
                    .then_inc(gate_ready, 1)

            def span_sums():
                pe.wait_ge(log_ready, 2)
                for k in range(8):
                    for tt in range(TT):
                        last = pe.matmul(aux[:, 0, k * 10:(k + 1) * 10], log_a[:, tt, k * P:(k + 1) * P],
                                         spans[:, tt, :], start=tt == 0, stop=tt == 1)
                last.then_inc(span_ready, 1)

            def suffix_sums(i):
                tt, half = divmod(i, 2)
                if i == 0:
                    pe.wait_ge(gate_out, 4)
                if i == 1:
                    pe.wait_ge(decay_ready, 1)
                if i >= 2:
                    pe.wait_ge(suf_out, i - 1)
                pe.matmul(aux[:, (i + 1) % 2, :], suffix[:, :], log_a[:, tt, half * N:(half + 1) * N],
                          start=True, stop=True).then_inc(suf_ready, 1)

            def turn_keys(g):
                g0 = groups_before(2)
                if g == 0:
                    pe.wait_ge(keys_ready, 2)
                group(g0, g, g0 + g - 1, lambda k, tt: keys[:, tt, (2 * g + k) * P:(2 * g + k + 1) * P])

            def gla_scores(hd):
                pe.wait_ge(sq_q, hd + 1)
                pe.wait_ge(tp_hi, groups_before(3))
                if hd >= 2:
                    pe.wait_ge(sc_act, hd - 1)
                    pe.wait_ge(sc_dve, hd - 1)
                for c in range(4):
                    width = (4 - c) * CHUNK
                    col = (c // 2) * S + c * CHUNK
                    off = (0, 8, 14, 18)[c] * CHUNK
                    rowp = (c % 2) * CHUNK
                    for k in range(2):
                        last = pe.matmul(
                            aux[rowp:rowp + CHUNK, hd % 2, col:col + width],
                            key_t[:, 2 * hd + k, c * CHUNK:(c + 1) * CHUNK],
                            scaled_q[:, hd % 2, off + k * width:off + (k + 1) * width],
                            start=k == 0, stop=k == 1)
                last.then_inc(sc_ready, 1)

            def gla_out(hd):
                pe.wait_ge(vals_act, hd + 1)
                pe.wait_ge(vals_dve, hd + 1)
                if hd == 0:
                    pe.wait_ge(sc_act, GH)
                    pe.wait_ge(sc_dve, GH)
                else:
                    pe.wait_ge(o_read, hd)
                pe.matmul(aux[:, 0, :], scores[:, hd, 0:P], vals[:, 0, :], start=True, stop=True)
                pe.matmul(aux[:, 1, :], scores[:, hd, P:2 * P], vals[:, 0, :], start=True, stop=False)
                pe.matmul(aux[:, 1, :], scores[:, hd, 2 * P:3 * P], vals[:, 1, :], start=False, stop=True)\
                    .then_inc(o_ready, 1)

            def lru_gates(b):
                pe.wait_ge(conv_ready, b // 4 + 1)
                if b >= 2:
                    pe.wait_ge(lru_th, b - 1)
                else:
                    pe.wait_ge(late_in, 48)
                for i in range(2):
                    last = pe.matmul(aux[:, b % 2, i * S:(i + 1) * S], lru_w[:, i, b, :],
                                     conv[:, b % 4, :], start=i == 0, stop=True, skip_group_check=True)
                last.then_inc(lru_mm, 1)

            def sb_logits(hd):
                if hd == 0:
                    pe.wait_ge(tp_hi, groups_before(55))
                    pe.wait_ge(tp_lo, groups_before(55))
                if hd >= 2:
                    pe.wait_ge(y_out, hd - 1)
                b = aux[:, hd % 2, :]
                pe.matmul(b[:, 0:S], k2_t[:, hd, 0:P], q2_t[:, hd, :], start=True, stop=False,
                          skip_group_check=True)
                pe.matmul(b[:, S:S + P], k2_t[:, hd, P:S], q2_t[:, hd, P:S], start=False, stop=False,
                          skip_group_check=True)
                pe.matmul(b[:, 0:P], ident[:, :], neg_mask[:, :], start=False, stop=False,
                          skip_group_check=True)
                pe.matmul(b[:, S:S + P], ident[:, :], neg_mask[:, :], start=False, stop=False,
                          skip_group_check=True).then_inc(z_ready, 1)

            def sb_breaks(hd):
                pe.wait_ge(sp_out, hd + 1)
                b = aux[:, hd % 2, :]
                s = soft_sp[:, hd % 2, :]
                pe.matmul(b[:, 0:384], below[:, :], s, start=False, stop=False, skip_group_check=True)
                pe.matmul(b[:, P:S], neg_ones[:, :], s[:, S:S + P], start=False, stop=True,
                          skip_group_check=True).then_inc(lw_ready, 1)

            def sb_values(hd):
                pe.wait_ge(w_out_s, hd + 1)
                pe.wait_ge(v2_act, hd // 4 + 1)
                pe.wait_ge(v2_dve, hd // 4 + 1)
                b = aux[:, hd % 2, :]
                w = wts[:, hd % 2, :]
                v = slice(hd * P, (hd + 1) * P)
                pe.matmul(b[:, 0:S], v2[:, 0, v], w[:, 0:S], start=True, stop=False, skip_group_check=True)
                pe.matmul(b[:, P:S], v2[:, 1, v], w[:, S:S + P], start=False, stop=True,
                          skip_group_check=True).then_inc(y_ready, 1)

            def after(t, c, it):
                prev = KINDS[t - 1] if t else ""
                late = 6 if prev in "KQ" else 3 if prev == "r" and t < FIRST_O else 2
                if t >= 1 and prev in "qroguDxlKQ" and c == late:
                    turn_panel(t, it)
                if t == 0:
                    if c == 0:
                        turn_x(2)
                        turn_x(3)
                    if 1 <= c <= 4:
                        turn_x(c + 3)
                    if c == 4:
                        pe.wait_ge(par_in, 16 * len(par_src))
                        pe.wait_ge(par_ready, 1)
                        pe.transpose(aux[:, 1, 0:P], rows[:, :], ident[:, :]).then_inc(par_turned, 1)
                    if c == 6:
                        gate_low()
                    if c == 7:
                        pe.wait_ge(par_ready, 2)
                        gate_up(0)
                        gate_up(1)
                if t == 1:
                    if c == 1:
                        gate_up(2)
                        gate_up(3)
                    if c == 6:
                        span_sums()
                if t == 2:
                    if c == 0:
                        suffix_sums(0)
                        suffix_sums(1)
                    if c == 2:
                        suffix_sums(2)
                        suffix_sums(3)
                    if c in (5, 7):
                        turn_keys(c - 5)
                        turn_keys(c - 4)
                if t in (3, 4) and c in (5, 7):
                    gla_scores((t - 3) * 2 + (c - 5) // 2)
                if prev == "v" and c == 2:
                    gla_out((t - 5) // 2)
                if t >= 2 and KINDS[t - 2] == "x" and c < 2:
                    b = 4 * (t - 2 - FIRST_X) + 2 * c
                    lru_gates(b)
                    lru_gates(b + 1)
                if 55 <= t <= 58 and c < 6:
                    (sb_logits, sb_breaks, sb_values)[c // 2](2 * (t - 55) + c % 2)

            def run(t, it=None):
                for c in range(CH):
                    multiply(t, c, it)
                    after(t, c, it)

            pe.wait_ge(pool_chain, 2)
            pe.wait_ge(norm_in, 16)
            pe.transpose(aux[:, 1, 0:KT], rows[0:KT, :], ident[0:KT, 0:KT]).then_inc(par_turned, 1)
            turn_x(0)
            turn_x(1)
            for t in range(FIRST_U + 1):
                run(t)
            with pe.Fori(0, MLP_BLOCKS - 1) as it:
                for t in range(FIRST_U + 1, FIRST_U + 1 + BODY):
                    run(t, it)
            for t in range(FIRST_U + 1 + BODY * (MLP_BLOCKS - 1), PANELS):
                run(t)

        def panel_done(eng, t, it):
            eng.wait_ge(chunk_used, at(lambda q: CH * q, t, it))

        @block.scalar
        def _(act):
            steps = [0]

            def link(ins):
                steps[0] += 1
                ins.then_inc(act_chain, 1)
                act.wait_ge(act_chain, steps[0])

            def split_hi(t, c, it):
                n = CH * t + RING + c
                if n >= CH * PANELS:
                    return
                act.wait_ge(raw_in[n % RING], at(lambda q: 16 * ((CH * q + RING + c) // RING + 1), t, it))
                act.wait_ge(chunk_used, at(lambda q: CH * q + c + 1, t, it))
                act.activation(w_hi[:, n % RING, :, :], raw[:, n % RING, :, :], ACT.Copy)\
                    .then_inc(hi_ready, 1)

            def split_x(g, bank, dst, k0, gain, wait):
                act.wait_ge(tp_ready, wait)
                if gain is None:
                    act.activation(dst[:, k0:k0 + 2, :].rearrange("p a b -> p (a b)"), tp[:, bank, :],
                                   ACT.Copy).then_inc(tp_hi, 1)
                    return
                for k in range(2):
                    ins = act.activation(dst[:, k0 + k, :], tp[:, bank, k * S:(k + 1) * S], ACT.Copy,
                                         scale=par[:, gain + k0 + k:gain + k0 + k + 1])
                ins.then_inc(tp_hi, 1)

            def move_first(dst, done, scale=1.0):
                act.wait_ge(tp_ready, done)
                act.activation(dst, tp[:, 0, :].rearrange("p (a b) -> p a b", b=S), ACT.Copy,
                               scale=scale).then_inc(tp_hi, 1)
                act.wait_ge(tp_hi, done)
                act.sem_inc(tp_hi, 1)

            def stage_half(t, dst, scale, signal, it=None):
                panel_done(act, t, it)
                act.activation(dst, acc[:, (t - 1) % 2, 0, :], ACT.Copy, scale=scale)\
                    .then_inc(acc_read_act, 1)
                act.wait_ge(acc_read_act, count("kqvruxKQVgl", t - 1))
                del signal

            def squares(src, tt, col, junk_to):
                act.activation(junk_to, src, ACT.Square, accum_out=sums[:, col:col + 1])\
                    .then_inc(sq_ready, 1)
                sq_count[0] += 1
                act.wait_ge(sq_ready, sq_count[0])

            sq_count = [0]

            def before(t, c, it):
                prev = KINDS[t - 1] if t else ""
                q = t - 1
                b = q % 2
                if c == 0 and t:
                    if prev == "k":
                        if q == 0:
                            act.wait_ge(r1_ready, 1)
                        panel_done(act, t, it)
                        act.activation(keys[:, 0, q * N:(q + 1) * N], acc[:, b, 0, :], ACT.Copy,
                                       scale=rs[:, ST_X, 0:1]).then_inc(acc_read_act, 1)
                    if prev == "q":
                        panel_done(act, t, it)
                        act.activation(stage[:, b, 0, :], acc[:, b, 0, :], ACT.Copy,
                                       scale=scl[:, R1S:R1S + 1]).then_inc(acc_read_act, 1)
                        act.wait_ge(acc_read_act, count("kqvruxKQVgl", q))
                        act.sem_inc(stage_act, 1)
                    if prev == "v":
                        hd = (t - 5) // 2
                        panel_done(act, t, it)
                        if hd == 0:
                            act.wait_ge(tp_hi, groups_before(3))
                        act.activation(vals[:, 0, :], acc[:, b, 0, :], ACT.Copy, scale=rs[:, ST_X, 0:1])\
                            .then_inc(acc_read_act, 1)
                        act.wait_ge(acc_read_act, count("kqvruxKQVgl", q))
                        act.sem_inc(vals_act, 1)
                    if prev in "rgl":
                        panel_done(act, t, it)
                        half = scl[:, R1H:R1H + 2] if prev == "r" else scl[:, R2H:R2H + 2]
                        tanh_to = th if prev == "r" else stage[:, b, :, :]
                        z_to = zt if prev == "r" else zt2
                        n_silu = count("rgl", q)
                        if n_silu > 1:
                            act.wait_ge(stage_dve, count("qruDxKQgl", q) - 1)
                        for tt in range(TT):
                            act.activation(z_to[:, tt, :], acc[:, b, tt, :], ACT.Copy,
                                           scale=half[:, tt:tt + 1])
                            last = act.activation(tanh_to[:, tt, :], acc[:, b, tt, :], ACT.Tanh,
                                                  scale=half[:, tt:tt + 1])
                        last.then_inc(silu_act, 1)
                        act.wait_ge(silu_act, n_silu)
                        act.sem_inc(acc_read_act, 1)
                    if prev == "u":
                        if t == FIRST_U + 1 and it is not None:
                            pass
                        panel_done(act, t, it)
                        act.wait_ge(rs_ready, ST_MLP + 1)
                        act.activation(stage[:, b, 0, :], acc[:, b, 0, :], ACT.Relu,
                                       scale=rs[:, ST_MLP, 0:1]).then_inc(acc_read_act, 1)
                        act.wait_ge(acc_read_act, at(lambda u: count("kqvruxKQVgl", u - 1), t, it))
                        act.sem_inc(stage_act, 1)
                    if prev in "xKQ":
                        if q == FIRST_X:
                            act.wait_ge(r2_ready, 1)
                        panel_done(act, t, it)
                        act.activation(stage[:, b, 0, :], acc[:, b, 0, :], ACT.Copy,
                                       scale=scl[:, R2:R2 + 1]).then_inc(acc_read_act, 1)
                        act.wait_ge(acc_read_act, count("kqvruxKQVgl", q))
                        act.sem_inc(stage_act, 1)
                    if prev == "V":
                        j = q - 54
                        panel_done(act, t, it)
                        act.activation(v2[:, 0, j * N:(j + 1) * N], acc[:, b, 0, :], ACT.Copy,
                                       scale=scl[:, R2:R2 + 1]).then_inc(acc_read_act, 1)
                        act.wait_ge(acc_read_act, count("kqvruxKQVgl", q))
                        act.sem_inc(v2_act, 1)
                if prev == "o" and c == 1:
                    j = q - FIRST_O
                    act.wait_ge(h_added, count("odD", q))
                    for tt in range(TT):
                        squares(h[:, tt, j * N:(j + 1) * N], tt, Q_M + 4 * tt + j, junk_h)
                if prev == "D" and c == 0:
                    j = q - FIRST_DL
                    act.wait_ge(h_added, count("odD", q))
                    for tt in range(TT):
                        squares(h[:, tt, j * N:(j + 1) * N], tt, Q_F + 4 * tt + j, junk_h)
                    act.sem_inc(h_squared, 1)
                if prev == "D" and c == 3:
                    j = q - FIRST_DL
                    act.wait_ge(stage_dve, count("qruDxKQgl", q))
                    for tt in range(TT):
                        squares(h[:, tt, j * N:(j + 1) * N], tt, Q_N + 4 * tt + j, junk_h)
                if prev and prev in "qrouDx" and c == (4 if prev == "r" and t < FIRST_O else 3):
                    for g in range(2):
                        G = at(lambda u: groups_before(u) + g + 1, t, it)
                        if prev == "q" and g == 0:
                            move_first(qry_t[:, 4 * (q - 2):4 * (q - 2) + 2, :], G)
                        if prev == "r":
                            split_x(None, g, xb_hi, 4 * ((t - 6) // 2) + 2 * g, None, G)
                        if prev == "o":
                            split_x(None, g, xa_hi, 4 * (q - FIRST_O) + 2 * g, C_MLP, G)
                        if prev == "u":
                            split_x(None, g, xb_hi, 4 * ((q - FIRST_U) % 4) + 2 * g, None, G)
                        if prev == "D":
                            split_x(None, g, xa_hi, 4 * (q - FIRST_DL) + 2 * g, C_N2, G)
                        if prev == "x" and g == 0:
                            if q == FIRST_X + 1:
                                act.wait_ge(conv_ready, 1)
                            move_first(lru_x[:, 0:2, PAD:PAD + S], G)
                if prev and prev in "gl" and c == (7 if q == 57 else 3):
                    for g in range(2):
                        k = 4 * (q - 56) + 2 * g
                        act.wait_ge(prod_out, 2 * (q - 56) + g + 1)
                        act.activation(xb_hi[:, k:k + 2, :].rearrange("p a b -> p (a b)"),
                                       prod[:, g, :], ACT.Copy).then_inc(tp_hi, 1)
                if c == 7 and prev and prev in "KQ":
                    k = 4 * ((q - 50) % 2)
                    if prev == "K":
                        move_first(k2_t[:, k:k + 2, :], groups_before(t) + 1)
                    else:
                        move_first(q2_t[:, k:k + 2, :], groups_before(t) + 1, qk_gain[:, 2:3])
                if t == 0:
                    if 2 <= c <= 5:
                        g = c + 2
                        split_x(None, g % 2, xa_hi, 2 * g, C_GLA, g + 1)
                    if c == 3:
                        act.wait_ge(wg_in, 16)
                        act.wait_ge(pool_chain, 3)
                        act.activation(gate_w[:, :, 0:RANK], wg_raw, ACT.Copy).then_inc(wg_hi, 1)
                    if c in (5, 6):
                        squares(h[:, c - 5, :], c - 5, Q_X + c - 5, junk)
                if t == 1:
                    if c in (2, 4):
                        if c == 2:
                            act.preload_act_table_set("natural_log_exp_and_others")
                        for tt in ((c - 2) // 2,):
                            act.wait_ge(gate_out, 2 * tt + 2)
                            z = z_gate[:, 2 * tt:2 * tt + 2, :].rearrange("p a b -> p (a b)")
                            link(act.activation(log_a[:, tt, :], z, ACT.Abs))
                            link(act.activation(log_a[:, tt, :], log_a[:, tt, :], ACT.Exp, scale=-1.0))
                            act.activation(log_a[:, tt, :], log_a[:, tt, :], ACT.Ln, bias=1.0)\
                                .then_inc(ln_ready, 1)
                    if c == 5:
                        act.wait_ge(par_ready, 2)
                        t0 = lru_par[:, L_T:L_T + 8]
                        link(act.activation(t0, par[:, C_LAM:C_LAM + 8], ACT.Abs))
                        link(act.activation(t0, t0, ACT.Exp, scale=-1.0))
                        act.activation(t0, t0, ACT.Ln, bias=1.0).then_inc(lam_act, 1)
                    if c == 7:
                        act.wait_ge(span_ready, 1)
                        act.activation(decay.rearrange("p a b -> p (a b)"), aux[:, 0, 0:80], ACT.Exp)\
                            .then_inc(decay_ready, 1)
                if t == 2:
                    if c in (1, 3):
                        for i in (c - 1, c):
                            tt, half = divmod(i, 2)
                            act.wait_ge(suf_ready, i + 1)
                            act.activation(log_a[:, tt, half * N:(half + 1) * N], aux[:, (i + 1) % 2, :],
                                           ACT.Exp).then_inc(suf_out, 1)
                    if c == 6:
                        move_first(key_t[:, 0:2, :], groups_before(2) + 1)
                if t == 3 and c == 1:
                    move_first(key_t[:, 4:6, :], groups_before(2) + 3)
                if (t, c) in ((3, 6), (4, 1), (4, 6), (5, 1)):
                    hd = ((3, 6), (4, 1), (4, 6), (5, 1)).index((t, c))
                    act.wait_ge(sc_ready, hd + 1)
                    act.activation(scores[0:64, hd, 0:S], aux[0:64, hd % 2, 0:S], ACT.Copy)
                    act.activation(scores[0:64, hd, S:S + P], aux[0:64, hd % 2, S + P:2 * S], ACT.Copy)\
                        .then_inc(sc_act, 1)
                if prev == "v" and c == 3:
                    hd = (t - 5) // 2
                    act.wait_ge(o_ready, hd + 1)
                    for tt in range(TT):
                        squares(aux[:, tt, :], tt, Q_O + 2 * hd + tt, junk_o)
                if t >= 2 and KINDS[t - 2] == "x" and c in (1, 2):
                    j = q - 1 - FIRST_X
                    for i in range(2):
                        blk = 4 * j + 2 * (c - 1) + i
                        act.wait_ge(lru_mm, blk + 1)
                        if blk == 4:
                            act.wait_ge(lru_done, 1)
                        if blk == 0:
                            act.wait_ge(lam_ready, 1)
                        act.activation(th_r[:, blk % 4, :], aux[:, blk % 2, 0:S], ACT.Tanh,
                                       bias=lru_par[:, L_BA + blk:L_BA + blk + 1], scale=0.5)
                        act.activation(th_i[:, blk % 4, :], aux[:, blk % 2, S:2 * S], ACT.Tanh,
                                       bias=lru_par[:, L_BX + blk:L_BX + blk + 1], scale=0.5)\
                            .then_inc(lru_th, 1)
                if t >= 2 and KINDS[t - 2] == "x":
                    j = q - 1 - FIRST_X
                    if c == 3:
                        act.wait_ge(lru_th, 4 * j + 4)
                        for i in range(4):
                            col = 4 * j + i
                            sp4 = lru_par[:, L_SP + col:L_SP + col + 1]
                            neg4 = lru_par[:, L_NEG + col:L_NEG + col + 1]
                            act.activation(lru_a[:, i, :], th_r[:, i, :], ACT.Exp, bias=neg4, scale=neg4)
                            last = act.activation(lru_u[:, i, :], th_r[:, i, :], ACT.Tanh, bias=sp4, scale=sp4)
                        last.then_inc(lru_exp, 1)
                    if c == 5:
                        act.wait_ge(lru_sq, j + 1)
                        act.activation(lru_u, lru_u, ACT.Sqrt, scale=0.25).then_inc(lru_root, 1)
                if prev and prev in "KQ" and c == 1:
                    act.wait_ge(kq_sq, q - 50 + 1)
                    act.activation(sq2, stage[:, b, :, :], ACT.Square).then_inc(kq_red, 1)
                if 55 <= t <= 58:
                    if c == 1:
                        act.preload_act_table_set("natural_log_exp_and_others")
                    if c in (1, 2):
                        hd = 2 * (t - 55) + c - 1
                        act.wait_ge(z_ready, hd + 1)
                        e = soft[:, hd % 2, :]
                        link(act.activation(e, aux[:, hd % 2, 0:384], ACT.Abs))
                        link(act.activation(e, e, ACT.Exp, scale=-1.0))
                        act.activation(e, e, ACT.Ln, bias=1.0).then_inc(ln_out, 1)
                    if c in (3, 4):
                        hd = 2 * (t - 55) + c - 3
                        act.wait_ge(lw_ready, hd + 1)
                        act.activation(wts[:, hd % 2, :], aux[:, hd % 2, 0:384], ACT.Exp)\
                            .then_inc(w_out_s, 1)

            def run(t, it=None):
                for c in range(CH):
                    before(t, c, it)
                    if t < PANELS:
                        split_hi(t, c, it)

            for j in range(4):
                act.dma_start(h[:, :, j * N:(j + 1) * N], x_v[:, :, j * N:(j + 1) * N])\
                    .then_inc(x_in[j], 16)
            act.dma_start(wg_raw, w_in_v[:, :, 2 * GH * GDK + 2 * D:]).then_inc(wg_in, 16)
            act.wait_ge(par_ready, 1)
            for n in range(RING):
                split_x(None, n % 2, xa_hi, 2 * n, C_GLA, n + 1)
                act.wait_ge(raw_in[n], 16)
                act.activation(w_hi[:, n, :, :], raw[:, n, :, :], ACT.Copy).then_inc(hi_ready, 1)
            for t in range(FIRST_U + 1):
                run(t)
            with act.Fori(0, MLP_BLOCKS - 1) as it:
                for t in range(FIRST_U + 1, FIRST_U + 1 + BODY):
                    run(t, it)
            for t in range(FIRST_U + 1 + BODY * (MLP_BLOCKS - 1), PANELS + 1):
                run(t)

        @block.vector
        def _(dve):
            steps = [0]

            def link(ins):
                steps[0] += 1
                ins.then_inc(dve_chain, 1)
                dve.wait_ge(dve_chain, steps[0])

            def split_lo(t, c, it):
                n = CH * t + RING + c
                if n >= CH * PANELS:
                    return
                dve.wait_ge(hi_ready, at(lambda q: CH * q + RING + c + 1, t, it))
                dve.tensor_tensor(w_lo[:, n % RING, :, :], raw[:, n % RING, :, :],
                                  w_hi[:, n % RING, :, :].bitcast(F32), ALU.subtract).then_inc(lo_ready, 1)

            def rest_x(bank, hi, lo, k0, gain, wait):
                dve.wait_ge(tp_hi, wait)
                if gain is None:
                    dve.tensor_tensor(lo[:, k0:k0 + 2, :].rearrange("p a b -> p (a b)"), tp[:, bank, :],
                                      hi[:, k0:k0 + 2, :].rearrange("p a b -> p (a b)").bitcast(F32),
                                      ALU.subtract).then_inc(tp_lo, 1)
                    return
                for k in range(2):
                    ins = dve.scalar_tensor_tensor(
                        out=lo[:, k0 + k, :], in0=tp[:, bank, k * S:(k + 1) * S],
                        scalar=par[:, gain + k0 + k:gain + k0 + k + 1],
                        in1=hi[:, k0 + k, :].bitcast(F32), op0=ALU.mult, op1=ALU.subtract)
                ins.then_inc(tp_lo, 1)

            def move_second(dst, done, scale=None):
                dve.wait_ge(tp_lo, done - 2)
                dve.sem_inc(tp_lo, 1)
                dve.wait_ge(tp_ready, done)
                src = tp[:, 1, :].rearrange("p (a b) -> p a b", b=S)
                if scale is None:
                    dve.tensor_copy(dst, src).then_inc(tp_lo, 1)
                else:
                    dve.tensor_scalar(dst, src, scale, None, ALU.mult).then_inc(tp_lo, 1)

            def mean(i, src, width):
                dve.tensor_scalar(ms[:, i, 0:ST_WIDTH[i]], src, 1.0 / width, EPS, ALU.mult, ALU.add)\
                    .then_inc(ms_ready, 1)

            def half_panel(t, it, dst, scale):
                panel_done(dve, t, it)
                dve.tensor_scalar(dst, acc[:, (t - 1) % 2, 1, :], scale, None, ALU.mult)\
                    .then_inc(acc_read_dve, 1)
                dve.wait_ge(acc_read_dve, count("kqvouDdxKQVf", t - 1))

            def scale_queries(hd):
                if hd >= 2:
                    dve.wait_ge(sc_ready, hd - 1)
                if hd % 2 == 0:
                    dve.wait_ge(tp_hi, groups_before(4 + hd // 2))
                    dve.wait_ge(tp_lo, groups_before(4 + hd // 2))
                for c in range(4):
                    n = 4 - c
                    off = (0, 8, 14, 18)[c] * CHUNK
                    dst = scaled_q[:, hd % 2, off:off + 2 * n * CHUNK]
                    d = decay[:, 2 * hd:2 * hd + 2, (0, 4, 7, 9)[c]:(0, 4, 7, 9)[c] + n]
                    ins = dve.tensor_tensor(
                        dst.rearrange("p (k n s) -> p k n s", k=2, n=n),
                        qry_t[:, 2 * hd:2 * hd + 2, c * CHUNK:S].rearrange("p k (n s) -> p k n s", n=n),
                        d.unsqueeze(3).to_broadcast([P, 2, n, CHUNK]), ALU.mult)
                ins.then_inc(sq_q, 1)

            def before(t, c, it):
                prev = KINDS[t - 1] if t else ""
                q = t - 1
                b = q % 2
                if c == 0 and t:
                    if prev == "k":
                        if q == 0:
                            dve.wait_ge(rs_ready, 1)
                        half_panel(t, it, keys[:, 1, q * N:(q + 1) * N], rs[:, ST_X, 1:2])
                    if prev == "q":
                        half_panel(t, it, stage[:, b, 1, :], scl[:, R1S + 1:R1S + 2])
                        dve.sem_inc(stage_dve, 1)
                    if prev == "v":
                        if q == 4:
                            dve.wait_ge(tp_hi, groups_before(3))
                        half_panel(t, it, vals[:, 1, :], rs[:, ST_X, 1:2])
                        dve.sem_inc(vals_dve, 1)
                    if prev == "r":
                        hd = (t - 6) // 2
                        dve.wait_ge(silu_act, hd + 1)
                        if hd == 0:
                            dve.wait_ge(gain_in, 48)
                        link(dve.scalar_tensor_tensor(out=th, in0=th, scalar=1.0, in1=zt,
                                                      op0=ALU.add, op1=ALU.mult))
                        link(dve.tensor_tensor(th, th, o_gain[:, :].unsqueeze(1).to_broadcast([P, TT, N]),
                                               ALU.mult))
                        dve.wait_ge(rs_ready, ST_O + hd + 1)
                        for tt in range(TT):
                            ins = dve.scalar_tensor_tensor(
                                out=stage[:, b, tt, :], in0=aux[:, tt, :],
                                scalar=rs[:, ST_O + hd, tt:tt + 1], in1=th[:, tt, :],
                                op0=ALU.mult, op1=ALU.mult)
                        ins.then_inc(o_read, 1)
                        dve.wait_ge(o_read, hd + 1)
                        dve.sem_inc(stage_dve, 1)
                    if prev and prev in "odD":
                        j = (q - (FIRST_O if prev == "o" else FIRST_U + 4)) % 4
                        panel_done(dve, t, it)
                        prior = at(lambda u: count("odD", u - 1) - 4, t, it)
                        if prev != "o":
                            dve.wait_ge(h_added, prior)
                        if prev == "o" and j == 0:
                            dve.wait_ge(sq_ready, 2)
                        dve.tensor_tensor(h[:, :, j * N:(j + 1) * N], h[:, :, j * N:(j + 1) * N],
                                          acc[:, b, :, :], ALU.add).then_inc(h_added, 1)
                        dve.wait_ge(h_added, at(lambda u: count("odD", u - 1), t, it))
                        dve.sem_inc(acc_read_dve, 1)
                    if prev == "u":
                        panel_done(dve, t, it)
                        dve.wait_ge(rs_ready, ST_MLP + 1)
                        dve.tensor_scalar(stage[:, b, 1, :], acc[:, b, 1, :], rs[:, ST_MLP, 1:2], 0.0,
                                          ALU.mult, ALU.max).then_inc(acc_read_dve, 1)
                        dve.wait_ge(acc_read_dve, at(lambda u: count("kqvouDdxKQVf", u - 1), t, it))
                        dve.wait_ge(stage_act, at(lambda u: count("quxKQ", u - 1), t, it))
                        dve.tensor_tensor(stage[:, b, :, :], stage[:, b, :, :], stage[:, b, :, :],
                                          ALU.mult).then_inc(stage_dve, 1)
                    if prev in "xKQ":
                        if q == FIRST_X:
                            dve.wait_ge(r2_ready, 1)
                        half_panel(t, it, stage[:, b, 1, :], scl[:, R2 + 1:R2 + 2])
                        if prev == "x":
                            dve.sem_inc(stage_dve, 1)
                        else:
                            dve.wait_ge(stage_act, count("quxKQ", q))
                            dve.sem_inc(kq_sq, 1)
                    if prev == "V":
                        j = q - 54
                        half_panel(t, it, v2[:, 1, j * N:(j + 1) * N], scl[:, R2 + 1:R2 + 2])
                        dve.sem_inc(v2_dve, 1)
                    if prev and prev in "gl":
                        dve.wait_ge(silu_act, count("rgl", q))
                        dve.scalar_tensor_tensor(out=stage[:, b, :, :], in0=stage[:, b, :, :], scalar=1.0,
                                                 in1=zt2, op0=ALU.add, op1=ALU.mult).then_inc(stage_dve, 1)
                    if prev == "f":
                        j = q - FIRST_F
                        panel_done(dve, t, it)
                        if j >= 2:
                            dve.wait_ge(out_sent[j % 2], 16 * TT)
                        for tt in range(TT):
                            dve.scalar_tensor_tensor(
                                out=stage[:, b, tt, :], in0=h[:, tt, j * N:(j + 1) * N],
                                scalar=rs[:, ST_FIN, tt:tt + 1], in1=acc[:, b, tt, :],
                                op0=ALU.mult, op1=ALU.add).then_inc(out_ready, 1)
                        dve.wait_ge(out_ready, TT * (j + 1))
                        dve.sem_inc(acc_read_dve, 1)
                if prev == "D" and c == 1:
                    j = q - FIRST_DL
                    if j == 0:
                        dve.wait_ge(late_in, 48)
                    dve.wait_ge(h_squared, j + 1)
                    dve.tensor_tensor(h[:, :, j * N:(j + 1) * N], h[:, :, j * N:(j + 1) * N],
                                      fin_gain[:, j * N:(j + 1) * N].unsqueeze(1).to_broadcast([P, TT, N]),
                                      ALU.mult).then_inc(stage_dve, 1)
                if prev and prev in "qrouDx" and c == (4 if prev == "r" and t < FIRST_O else 3):
                    for g in range(2):
                        G = at(lambda u: groups_before(u) + g + 1, t, it)
                        if prev == "q" and g == 1:
                            move_second(qry_t[:, 4 * (q - 2) + 2:4 * (q - 2) + 4, :], G)
                        if prev == "r":
                            rest_x(g, xb_hi, xb_lo, 4 * ((t - 6) // 2) + 2 * g, None, G)
                        if prev == "o":
                            rest_x(g, xa_hi, xa_lo, 4 * (q - FIRST_O) + 2 * g, C_MLP, G)
                        if prev == "u":
                            rest_x(g, xb_hi, xb_lo, 4 * ((q - FIRST_U) % 4) + 2 * g, None, G)
                        if prev == "D":
                            rest_x(g, xa_hi, xa_lo, 4 * (q - FIRST_DL) + 2 * g, C_N2, G)
                        if prev == "x" and g == 1:
                            if q == FIRST_X:
                                link(dve.memset(lru_x[:, :, 0:PAD], 0.0))
                            move_second(lru_x[:, 2:4, PAD:PAD + S], G)
                if prev and prev in "gl" and c == (7 if q == 57 else 3):
                    mixed = y_t if prev == "g" else lru_h
                    k0 = 4 * ((q - 56) % 2)
                    if prev == "g":
                        dve.wait_ge(y_out, k0 + 4)
                    else:
                        dve.wait_ge(lru_done, 2)
                    for g in range(2):
                        dve.wait_ge(tp_ready, groups_before(t) + g + 1)
                        if q > 56:
                            dve.wait_ge(tp_lo, groups_before(t))
                        dve.tensor_tensor(prod[:, g, :], tp[:, g, :],
                                          mixed[:, k0 + 2 * g:k0 + 2 * g + 2, :].rearrange("p a b -> p (a b)"),
                                          ALU.mult).then_inc(prod_out, 1)
                    for g in range(2):
                        k = 4 * (q - 56) + 2 * g
                        dve.wait_ge(tp_hi, groups_before(t) + g + 1)
                        dve.tensor_tensor(xb_lo[:, k:k + 2, :].rearrange("p a b -> p (a b)"), prod[:, g, :],
                                          xb_hi[:, k:k + 2, :].rearrange("p a b -> p (a b)").bitcast(F32),
                                          ALU.subtract).then_inc(tp_lo, 1)
                if c == 7 and prev and prev in "KQ":
                    k = 4 * ((q - 50) % 2) + 2
                    if prev == "K":
                        move_second(k2_t[:, k:k + 2, :], groups_before(t) + 2)
                    else:
                        move_second(q2_t[:, k:k + 2, :], groups_before(t) + 2, qk_gain[:, 2:3])
                if t == FIRST_U and c == 2:
                    dve.wait_ge(sq_ready, 18)
                    link(dve.tensor_reduce(scl[:, T0:T0 + 2],
                                           sums[:, Q_M:Q_M + 8].rearrange("p (t j) -> p t j", j=4),
                                           AX.X, ALU.add))
                    mean(ST_MLP, scl[:, T0:T0 + 2], D)
                if t == FIRST_X and c == 4:
                    dve.wait_ge(sq_ready, 34)
                    link(dve.tensor_reduce(scl[:, T0:T0 + 2],
                                           sums[:, Q_F:Q_F + 8].rearrange("p (t j) -> p t j", j=4),
                                           AX.X, ALU.add))
                    mean(ST_FIN, scl[:, T0:T0 + 2], D)
                    link(dve.tensor_reduce(scl[:, T1:T1 + 2],
                                           sums[:, Q_N:Q_N + 8].rearrange("p (t j) -> p t j", j=4),
                                           AX.X, ALU.add))
                if t == FIRST_X and c == 6:
                    dve.wait_ge(rs_ready, ST_FIN + 1)
                    rf = rs[:, ST_FIN, 0:2]
                    link(dve.tensor_tensor(scl[:, RF2:RF2 + 2], rf, rf, ALU.mult))
                    link(dve.tensor_tensor(scl[:, T1:T1 + 2], scl[:, T1:T1 + 2], scl[:, RF2:RF2 + 2],
                                           ALU.mult))
                    mean(ST_N2, scl[:, T1:T1 + 2], D)
                if t == FIRST_X and c == 7:
                    dve.wait_ge(rs_ready, ST_N2 + 1)
                    link(dve.tensor_tensor(scl[:, R2:R2 + 2], rs[:, ST_FIN, 0:2], rs[:, ST_N2, 0:2],
                                           ALU.mult))
                    dve.tensor_scalar(scl[:, R2H:R2H + 2], scl[:, R2:R2 + 2], 0.5, None, ALU.mult)\
                        .then_inc(r2_ready, 1)
                if t == 0:
                    if 2 <= c <= 5:
                        g = c + 2
                        rest_x(g % 2, xa_hi, xa_lo, 2 * g, C_GLA, g + 1)
                    if c == 4:
                        dve.wait_ge(wg_hi, 1)
                        dve.tensor_tensor(gate_w[:, :, 32:32 + RANK], wg_raw,
                                          gate_w[:, :, 0:RANK].bitcast(F32), ALU.subtract).then_inc(wg_lo, 1)
                    if c == 5:
                        dve.wait_ge(par_turned, 2)
                        dve.tensor_copy(par[:, KT:P], aux[:, 1, KT:P]).then_inc(par_ready, 1)
                    if c == 7:
                        dve.wait_ge(low_ready, 1)
                        dve.tensor_copy(g_low, aux[:, 0, 0:S]).then_inc(low_out, 1)
                        dve.wait_ge(sq_ready, 2)
                        mean(ST_X, sums[:, Q_X:Q_X + 2], D)
                if t == 1 and c == 0:
                    dve.wait_ge(rs_ready, 1)
                    dve.tensor_scalar(scl[:, R1S:R1S + 2], rs[:, ST_X, 0:2], GDK ** -0.5, None, ALU.mult)
                    link(dve.tensor_scalar(scl[:, R1H:R1H + 2], rs[:, ST_X, 0:2], 0.5, None, ALU.mult))
                    dve.sem_inc(r1_ready, 1)
                if t == 1:
                    if c in (1, 2):
                        for i in (2 * c - 2, 2 * c - 1):
                            tt, half = divmod(i, 2)
                            dve.wait_ge(gate_ready, i + 1)
                            dve.scalar_tensor_tensor(
                                out=z_gate[:, i, :], in0=aux[:, (i + 1) % 2, :],
                                scalar=rs[:, ST_X, tt:tt + 1], in1=b_gate[:, half * N:(half + 1) * N],
                                op0=ALU.mult, op1=ALU.add).then_inc(gate_out, 1)
                    if c in (4, 6):
                        tt = (c - 4) // 2
                        dve.wait_ge(ln_ready, tt + 1)
                        dve.wait_ge(gate_out, 4)
                        dve.scalar_tensor_tensor(
                            out=log_a[:, tt, :],
                            in0=z_gate[:, 2 * tt:2 * tt + 2, :].rearrange("p a b -> p (a b)"),
                            scalar=0.0, in1=log_a[:, tt, :], op0=ALU.min, op1=ALU.subtract)\
                            .then_inc(log_ready, 1)
                if t == 2:
                    if c == 1:
                        dve.wait_ge(lam_act, 1)
                        lam = par[:, C_LAM:C_LAM + 8]
                        link(dve.tensor_scalar(lru_par[:, L_SP:L_SP + 8], lam, -1.0, 0.0, ALU.mult, ALU.max))
                        link(dve.tensor_tensor(lru_par[:, L_SP:L_SP + 8], lru_par[:, L_SP:L_SP + 8],
                                               lru_par[:, L_T:L_T + 8], ALU.add))
                        link(dve.tensor_scalar(lru_par[:, L_SP:L_SP + 8], lru_par[:, L_SP:L_SP + 8],
                                               LRU_C / 2, None, ALU.mult))
                        link(dve.tensor_scalar(lru_par[:, L_NEG:L_NEG + 8], lru_par[:, L_SP:L_SP + 8],
                                               -1.0, None, ALU.mult))
                        dve.wait_ge(gain_in, 48)
                        link(dve.tensor_scalar(lru_par[:, L_BA:L_BA + 16], par[:, C_BA:C_BA + 16], 0.5,
                                               None, ALU.mult))
                        dve.scalar_tensor_tensor(out=qk_gain[:, 2:3], in0=qk_gain[:, 0:1],
                                                 scalar=HD ** -0.5, in1=qk_gain[:, 1:2],
                                                 op0=ALU.mult, op1=ALU.mult).then_inc(lam_ready, 1)
                    if c in (2, 4):
                        tt = c // 2 - 1
                        dve.wait_ge(suf_out, c)
                        dve.wait_ge(acc_read_act, 2)
                        dve.tensor_tensor(keys[:, tt, :], keys[:, tt, :], log_a[:, tt, :], ALU.mult)\
                            .then_inc(keys_ready, 1)
                    if c == 6:
                        move_second(key_t[:, 2:4, :], groups_before(2) + 2)
                if t == 3 and c == 1:
                    move_second(key_t[:, 6:8, :], groups_before(2) + 4)
                    for a in (0, S):
                        dve.memset(scores[64:128, :, a:a + 64], 0.0)
                if (t, c) in ((3, 4), (3, 6), (4, 4), (4, 6)):
                    scale_queries(((3, 4), (3, 6), (4, 4), (4, 6)).index((t, c)))
                if (t, c) in ((3, 6), (4, 1), (4, 6), (5, 1)):
                    hd = ((3, 6), (4, 1), (4, 6), (5, 1)).index((t, c))
                    dve.wait_ge(sc_ready, hd + 1)
                    dve.tensor_copy(scores[64:128, hd, 64:S], aux[64:128, hd % 2, 64:S])
                    dve.tensor_copy(scores[64:128, hd, S + 64:S + P], aux[64:128, hd % 2, 2 * S - 64:2 * S])\
                        .then_inc(sc_dve, 1)
                if prev == "v" and c == 4:
                    hd = (t - 5) // 2
                    dve.wait_ge(sq_ready, 2 + 2 * hd + 2)
                    mean(ST_O + hd, sums[:, Q_O + 2 * hd:Q_O + 2 * hd + 2], N)
                if prev == "x" and c in (5, 6):
                    j = q - FIRST_X
                    if c == 5:
                        dve.wait_ge(tp_hi, groups_before(t + 1))
                        dve.wait_ge(tp_lo, groups_before(t + 1))
                    if c == 5 and j == 1:
                        dve.wait_ge(lru_mm, 4)
                    for w in ((3, 2) if c == 5 else (1, 0)):
                        for i in range(4):
                            col = C_CONV + 8 * w + 4 * j + i
                            wcol = par[:, col:col + 1]
                            if w == 3:
                                ins = dve.tensor_scalar(
                                    conv[:, i, :], lru_x[:, i, w:w + S], wcol,
                                    par[:, C_CB + 4 * j + i:C_CB + 4 * j + i + 1], ALU.mult, ALU.add)
                            else:
                                ins = dve.scalar_tensor_tensor(
                                    out=conv[:, i, :], in0=lru_x[:, i, w:w + S], scalar=wcol,
                                    in1=conv[:, i, :], op0=ALU.mult, op1=ALU.add)
                        if w:
                            link(ins)
                        else:
                            ins.then_inc(conv_ready, 1)
                if t >= 2 and KINDS[t - 2] == "x":
                    j = q - 1 - FIRST_X
                    if c == 3:
                        dve.wait_ge(lru_th, 4 * j + 4)
                        link(dve.scalar_tensor_tensor(out=th_i, in0=th_i, scalar=1.0, in1=conv,
                                                      op0=ALU.add, op1=ALU.mult))
                    if c == 4:
                        dve.wait_ge(lru_exp, j + 1)
                        link(dve.tensor_tensor(th_r, lru_a, lru_a, ALU.mult))
                        dve.scalar_tensor_tensor(out=lru_u, in0=th_r, scalar=1.0, in1=lru_u,
                                                 op0=ALU.add, op1=ALU.mult).then_inc(lru_sq, 1)
                    if c == 7:
                        dve.wait_ge(lru_root, j + 1)
                        link(dve.tensor_tensor(th_i, lru_u, th_i, ALU.mult))
                        for i in range(4):
                            ins = dve.tensor_tensor_scan(lru_h[:, 4 * j + i, :], lru_a[:, i, :],
                                                         th_i[:, i, :], 0.0, ALU.mult, ALU.add)
                        ins.then_inc(lru_done, 1)
                if prev and prev in "KQ":
                    i = q - 50
                    if c == 2:
                        dve.wait_ge(kq_red, i + 1)
                        s8 = sums[:, Q_KQ + 8 * i:Q_KQ + 8 * i + 8]
                        link(dve.tensor_reduce(s8.rearrange("p (t n) -> p t n", n=4),
                                               sq2.rearrange("p t (n d) -> p t n d", d=HD), AX.X, ALU.add))
                        mean(ST_KQ + i, s8, HD)
                    if c == 3:
                        dve.wait_ge(rs_ready, ST_KQ + i + 1)
                        st = stage[:, b, :, :].rearrange("p t (n d) -> p (t n) d", d=HD)
                        dve.tensor_tensor(st, st, rs[:, ST_KQ + i, :].unsqueeze(2).to_broadcast([P, 8, HD]),
                                          ALU.mult).then_inc(stage_dve, 1)
                if 55 <= t <= 58:
                    if c in (1, 2):
                        hd = 2 * (t - 55) + c - 1
                        dve.wait_ge(ln_out, hd + 1)
                        dve.scalar_tensor_tensor(out=soft_sp[:, hd % 2, :], in0=aux[:, hd % 2, 0:384],
                                                 scalar=0.0, in1=soft[:, hd % 2, :], op0=ALU.max,
                                                 op1=ALU.add).then_inc(sp_out, 1)
                    if c in (5, 6):
                        hd = 2 * (t - 55) + c - 5
                        dve.wait_ge(y_ready, hd + 1)
                        dve.tensor_copy(y_t[:, hd, :], aux[:, hd % 2, 0:S]).then_inc(y_out, 1)

            def run(t, it=None):
                for c in range(CH):
                    before(t, c, it)
                    if t < PANELS:
                        split_lo(t, c, it)

            dve.wait_ge(par_turned, 1)
            dve.tensor_copy(par[:, 0:KT], aux[:, 1, 0:KT]).then_inc(par_ready, 1)
            dve.wait_ge(par_ready, 1)
            for n in range(RING):
                rest_x(n % 2, xa_hi, xa_lo, 2 * n, C_GLA, n + 1)
                dve.wait_ge(hi_ready, n + 1)
                dve.tensor_tensor(w_lo[:, n, :, :], raw[:, n, :, :], w_hi[:, n, :, :].bitcast(F32),
                                  ALU.subtract).then_inc(lo_ready, 1)
            for t in range(FIRST_U + 1):
                run(t)
            with dve.Fori(0, MLP_BLOCKS - 1) as it:
                for t in range(FIRST_U + 1, FIRST_U + 1 + BODY):
                    run(t, it)
            for t in range(FIRST_U + 1 + BODY * (MLP_BLOCKS - 1), PANELS + 1):
                run(t)


_INS = ["x", "gla_norm", "gla_w_in", "gla_w_gate_up", "gla_b_gate", "gla_o_norm", "gla_w_out",
        "mlp_norm", "mlp_w_up", "mlp_w_down", "final_norm", "norm_gain_2", "w_in_2",
        "q_norm_gain_2", "k_norm_gain_2", "conv_w_2", "conv_b_2", "lru_w_a_2", "lru_b_a_2",
        "lru_w_x_2", "lru_b_x_2", "lru_lambda_2", "w_out_2"]
_OUT = (1, S, D)


def kernel(**inputs):
    import numpy as np
    import concourse.bacc as bacc
    from concourse.bass_utils import run_bass_kernel_spmd as run

    nc = bacc.Bacc("TRN2", target_bir_lowering=False, num_devices=1)
    arrays, args = {}, []
    for name in _INS:
        a = np.ascontiguousarray(inputs[name])
        arrays[f"in_{name}"] = a
        args.append(nc.dram_tensor(f"in_{name}", a.shape, F32, kind="ExternalInput").ap())
    out = nc.dram_tensor("result", _OUT, F32, kind="ExternalOutput").ap()
    gated_block_kernel(nc, *args, out)
    return run(nc, [arrays], core_ids=[0]).results[0]["result"]
```

```python
import concourse.bass as bass
from concourse import mybir
from contextlib import ExitStack

F32 = mybir.dt.float32
F32R = mybir.dt.float32r
ALU = mybir.AluOpType
ACT = mybir.ActivationFunctionType
AX = mybir.AxisListType

P = 128
D = 2048
S = 256
TT = S // P
KT = D // P
N = 512
CK = 2
CH = KT // CK
RING = 4
EPS = 1e-6
CHUNK = 64
GH = 4
GDK = 256
RANK = 16
HD = 128
SH = 8
LRU_C = 8.0
CONV = 4
MLP_BLOCKS = 4

KINDS = "kkqq" + "vr" * GH + "oooo" + ("uuuu" + "dddd") * (MLP_BLOCKS - 1) + "uuuuDDDD" \
    + "xxKKQQVVggll" + "ffff"
PANELS = len(KINDS)
FIRST_Q = KINDS.index("q")
FIRST_V = KINDS.index("v")
FIRST_R = KINDS.index("r")
FIRST_O = KINDS.index("o")
FIRST_U = KINDS.index("u")
FIRST_DL = KINDS.index("D")
FIRST_X = KINDS.index("x")
FIRST_K2 = KINDS.index("K")
FIRST_V2 = KINDS.index("V")
FIRST_G = KINDS.index("g")
FIRST_F = KINDS.index("f")
ATTEND = FIRST_V2 + 1
ATTEND_END = ATTEND + SH // 2
BODY = 8

ST_X, ST_O, ST_MLP, ST_FIN, ST_N2, ST_KQ, ST_ALL = 0, 1, 5, 6, 7, 8, 12
ST_WIDTH = [TT] * ST_KQ + [TT * 4] * (ST_ALL - ST_KQ)

DECAYS = ((3, 4), (3, 6), (4, 4), (4, 6))
SCORES_OUT = ((3, 6), (4, 1), (4, 6), (5, 1))
CONV_TAPS = ({5: (3, 2), 6: (1, 0)}, {5: (3,), 6: (2,), 8: (1,), 9: (0,)})


def count(kinds, p):
    return sum(k in kinds for k in KINDS[:p + 1])


def groups_before(turn):
    turned = sum(KINDS[q] in "qrouDxKQgl" for q in range(min(turn - 1, PANELS)))
    return CH + (4 if turn > 2 else 0) + 2 * turned


def lru_step(t, c, j):
    return CH * (t - FIRST_X - 2 - j) + c - 8 * j


def at(f, t, it):
    v = f(t)
    if it is None:
        return v
    step = f(t + BODY) - v
    assert f(t + 2 * BODY) - f(t + BODY) == step
    return it * step + v if step else v


def gated_block_kernel(nc, x, gla_norm, gla_w_in, gla_w_gate_up, gla_b_gate, gla_o_norm, gla_w_out,
                       mlp_norm, mlp_w_up, mlp_w_down, final_norm, norm_gain_2, w_in_2,
                       q_norm_gain_2, k_norm_gain_2, conv_w_2, conv_b_2, lru_w_a_2, lru_b_a_2,
                       lru_w_x_2, lru_b_x_2, lru_lambda_2, w_out_2, out):
    ctx = ExitStack()
    with ctx:
        def sb(name, shape, dt=F32):
            return ctx.enter_context(nc.sbuf_tensor(name, shape, dt))

        def sem(name):
            return ctx.enter_context(nc.semaphore(name))

        raw = sb("raw", [P, RING, CK, N])
        w_hi = sb("w_hi", [P, RING, CK, N], F32R)
        w_lo = sb("w_lo", [P, RING, CK, N], F32R)
        xa_hi = sb("xa_hi", [P, KT, S], F32R)
        xa_lo = sb("xa_lo", [P, KT, S], F32R)
        xb_hi = sb("xb_hi", [P, KT, S], F32R)
        xb_lo = sb("xb_lo", [P, KT, S], F32R)
        h = sb("h", [P, TT, D])
        stage = sb("stage", [P, 2, TT, N])
        ident = sb("ident", [P, P])
        suffix = sb("suffix", [P, P])
        ident_r = sb("ident_r", [P, P], F32R)
        below = sb("below", [P, P], F32R)
        neg_ones = sb("neg_ones", [P, P], F32R)
        neg_mask = sb("neg_mask", [P, P], F32R)
        spans = sb("spans", [P, TT, 7])
        neg_half = sb("neg_half", [P, 8])
        rows = sb("rows", [P, P])
        par = sb("par", [P, P])
        qk_gain = sb("qk_gain", [P, 4])
        o_gain = sb("o_gain", [P, N])
        sums = sb("sums", [P, 80])
        ms = sb("ms", [P, ST_ALL, 8])
        rs = sb("rs", [P, ST_ALL, 8])
        scl = sb("scl", [P, 20])
        lru_par = sb("lru_par", [P, 40])
        ARENA = 16384
        arena_at = (nc.sbuf_usable_end - 4 * ARENA) // 64 * 64
        arena = nc.alloc_sbuf_tensor_at("arena", [P, ARENA], F32, offset=arena_at)
        gate_w = nc.alloc_sbuf_tensor_at("gate_w", [P, KT, P], F32R,
                                         offset=arena_at + 4 * (ARENA - KT * P))
        assert nc.sbuf_base <= arena_at

        def room(start, *dims):
            size = 1
            for n in dims:
                size *= n
            v = arena[:, start:start + size]
            if len(dims) == 2:
                v = v.rearrange("p (a b) -> p a b", b=dims[1])
            if len(dims) == 3:
                v = v.rearrange("p (a b c) -> p a b c", b=dims[1], c=dims[2])
            return v

        log_a = room(0, TT, 1024)
        z_gate = room(2048, 4, N)
        b_gate = room(4096, 1024)
        w_up_gate = room(5120, 1024)
        g_low = room(6144, S)
        wg_raw = room(6400, KT, RANK)
        far_q = room(0, 2, 2, 3 * CHUNK)
        key_s = room(768, 8, S)
        scores = room(2816, GH, 384)
        zt = room(4352, TT, N)
        keys = room(6656, TT, 1024)
        vals = room(6656, TT, N)
        th = room(7680, TT, N)
        key_t = room(8704, 8, S)
        qry_t = room(10752, 8, S)
        decay = room(12800, 8, 7)
        junk = room(8704, D)
        junk_o = room(12900, N)
        draft = room(13500, 2, P)
        fin_gain = room(8192, D)
        junk_h = room(10240, N)
        lru_w = room(0, 2, 8, P)
        v2 = room(0, TT, 1024)
        q2_t = room(2048, 8, S)
        k2_t = room(4096, 8, S)
        lru_h = room(6144, 8, S)
        PAD = CONV - 1
        lru_x = room(8192, 4, PAD + S)
        conv = room(9228, 4, S)
        th_r = room(10252, 4, S)
        th_i = room(11276, 4, S)
        lru_a = room(12300, 4, S)
        lru_u = room(13324, 4, S)
        y_t = room(8192, 8, S)
        soft = room(10240, 2, 384)
        soft_sp = room(11008, 2, 384)
        sp_hi = nc.alloc_sbuf_tensor_at("sp_hi", [P, 2, 384], F32R, offset=arena_at + 4 * 15616)
        sp_lo = nc.alloc_sbuf_tensor_at("sp_lo", [P, 2, 384], F32R, offset=arena_at + 4 * 14592)
        wts = room(11776, 2, 384)
        zt2 = room(12544, TT, N)
        prod = room(13568, 2, N)
        sq2 = room(14592, TT, N)

        acc = ctx.enter_context(nc.psum_tensor("acc", [P, 2, TT, N], F32))
        tp = ctx.enter_context(nc.psum_tensor("tp", [P, 2, N], F32))
        aux = ctx.enter_context(nc.psum_tensor("aux", [P, 2, N], F32))

        raw_in = [sem(f"raw_in{i}") for i in range(RING)]
        hi_ready, lo_ready = sem("hi_ready"), sem("lo_ready")
        chunk_used = sem("chunk_used")
        acc_read_act, acc_read_dve = sem("acc_read_act"), sem("acc_read_dve")
        stage_act, stage_dve = sem("stage_act"), sem("stage_dve")
        tp_ready = sem("tp_ready")
        tp_hi, tp_lo = sem("tp_hi"), sem("tp_lo")
        norm_in = sem("norm_in")
        par_in, par_turned, par_ready = sem("par_in"), sem("par_turned"), sem("par_ready")
        x_in = [sem(f"x_in{i}") for i in range(4)]
        gain_in, up_in, wg_in = sem("gain_in"), sem("up_in"), sem("wg_in")
        consts, pool_chain = sem("consts"), sem("pool_chain")
        ms_ready, rs_ready = sem("ms_ready"), sem("rs_ready")
        sq_ready = sem("sq_ready")
        act_chain, dve_chain = sem("act_chain"), sem("dve_chain")
        wg_hi, wg_lo = sem("wg_hi"), sem("wg_lo")
        low_ready, low_out = sem("low_ready"), sem("low_out")
        gate_ready, gate_out = sem("gate_ready"), sem("gate_out")
        ln_ready, log_ready = sem("ln_ready"), sem("log_ready")
        span_ready, decay_ready = sem("span_ready"), sem("decay_ready")
        suf_ready, suf_out = sem("suf_ready"), sem("suf_out")
        keys_ready = sem("keys_ready")
        r1_ready = sem("r1_ready")
        sq_q, sc_ready, sc_act, sc_dve = sem("sq_q"), sem("sc_ready"), sem("sc_act"), sem("sc_dve")
        vals_act, vals_dve = sem("vals_act"), sem("vals_dve")
        o_ready, o_read = sem("o_ready"), sem("o_read")
        silu_act = sem("silu_act")
        h_added = sem("h_added")
        h_squared = sem("h_squared")
        late_in = sem("late_in")
        r2_ready = sem("r2_ready")
        lam_act, lam_ready = sem("lam_act"), sem("lam_ready")
        conv_ready = sem("conv_ready")
        lru_mm, lru_th = sem("lru_mm"), sem("lru_th")
        lru_exp, lru_sq, lru_root, lru_done = sem("lru_exp"), sem("lru_sq"), sem("lru_root"), sem("lru_done")
        kq_sq, kq_red = sem("kq_sq"), sem("kq_red")
        v2_act, v2_dve = sem("v2_act"), sem("v2_dve")
        z_ready, ln_out, sp_out = sem("z_ready"), sem("ln_out"), sem("sp_out")
        lw_ready, w_out_s, y_ready, y_out = sem("lw_ready"), sem("w_out_s"), sem("y_ready"), sem("y_out")
        prod_out = sem("prod_out")
        out_ready = sem("out_ready")
        out_sent = [sem(f"out_sent{i}") for i in range(2)]

        def tiles(w):
            return w.rearrange("(k p) n -> p k n", p=P)

        w_in_v, w_out_v = tiles(gla_w_in[0]), tiles(gla_w_out[0])
        up_v, down_v = tiles(mlp_w_up[0]), tiles(mlp_w_down[0])
        in2_v, out2_v = tiles(w_in_2[0]), tiles(w_out_2[0])
        x_v = x[0].rearrange("(t p) d -> p t d", p=P)
        out_v = out[0].rearrange("(t p) d -> p t d", p=P)

        par_src = [(mlp_norm[0], 16), (final_norm, 16), (norm_gain_2[0], 16),
                   (conv_w_2[0], 32), (lru_lambda_2[0], 8), (lru_b_a_2[0], 8), (lru_b_x_2[0], 8),
                   (conv_b_2[0], 8)]
        C_GLA, C_MLP, C_N2, C_CONV, C_LAM, C_BA, C_BX, C_CB = 0, 16, 48, 64, 96, 104, 112, 120
        R1S, R1H, R2, R2H, RF2, T0, T1 = 0, 2, 4, 6, 8, 10, 12
        Q_X, Q_O, Q_M, Q_F, Q_N, Q_KQ = 0, 2, 10, 18, 26, 40
        L_SP, L_NEG, L_BA, L_BX, L_T = 0, 8, 16, 24, 32

        block = ctx.enter_context(nc.Block())

        @block.sync
        def _(sp):
            def load(c, n0, it, per, src):
                n = n0 + c
                if it is None:
                    if n >= RING:
                        sp.wait_ge(lo_ready, n - RING + 1)
                elif n >= RING:
                    sp.wait_ge(lo_ready, it * per + (n - RING + 1))
                sp.dma_start(raw[:, n % RING, :, :], src).then_inc(raw_in[n % RING], 16)

            def panel(n0, it, per, view, row, col):
                for c in range(CH):
                    load(c, n0, it, per, view[:, bass.ds(row + CK * c, CK), bass.ds(col, N)])

            sp.dma_start(rows[0:KT, :], gla_norm[0].rearrange("(b p) -> b p", p=P)).then_inc(norm_in, 16)
            for c in range(RING):
                load(c, 0, None, CH, w_in_v[:, CK * c:CK * c + CK, GH * GDK:GH * GDK + N])
            for j in (2, 3):
                sp.dma_start(h[:, :, j * N:(j + 1) * N], x_v[:, :, j * N:(j + 1) * N])\
                    .then_inc(x_in[j], 16)
            sp.dma_start(wg_raw, w_in_v[:, :, 2 * GH * GDK + 2 * D:]).then_inc(wg_in, 16)
            for c in range(RING, CH):
                load(c, 0, None, CH, w_in_v[:, CK * c:CK * c + CK, GH * GDK:GH * GDK + N])
            panel(CH, None, CH, w_in_v, 0, GH * GDK + N)
            n = 2 * CH
            with sp.Fori(0, 2) as j:
                panel(n, j, CH, w_in_v, 0, j * N)
            n += 2 * CH
            with sp.Fori(0, GH) as j:
                panel(n, j, 2 * CH, w_in_v, 0, j * N + 2 * GH * GDK)
                panel(n + CH, j, 2 * CH, w_in_v, 0, j * N + 2 * GH * GDK + D)
            n += 2 * GH * CH
            with sp.Fori(0, 4) as j:
                panel(n, j, CH, w_out_v, 0, j * N)
            n += 4 * CH
            for b in range(MLP_BLOCKS):
                with sp.Fori(0, 4) as j:
                    panel(n, j, CH, up_v, 0, j * N + b * D)
                n += 4 * CH
                with sp.Fori(0, 4) as j:
                    panel(n, j, CH, down_v, b * KT, j * N)
                n += 4 * CH
            for first in (4096, 1024, 0, 2048, 3072, 5120):
                with sp.Fori(0, 2) as j:
                    panel(n, j, CH, in2_v, 0, j * N + first)
                n += 2 * CH
            with sp.Fori(0, 4) as j:
                panel(n, j, CH, out2_v, 0, j * N)
            for j in range(4):
                for tt in range(TT):
                    sp.wait_ge(out_ready, TT * j + tt + 1)
                    sp.dma_start(out_v[:, tt, j * N:(j + 1) * N], stage[:, j % 2, tt, :])\
                        .then_inc(out_sent[j % 2], 16)
            for s in out_sent:
                sp.wait_ge(s, 16 * TT * 2)

        @block.gpsimd
        def _(pool):
            steps = [0]

            def link(ins):
                steps[0] += 1
                ins.then_inc(pool_chain, 1)
                pool.wait_ge(pool_chain, steps[0])

            def triangle(m, value, op, base=0):
                link(pool.memset(m, value))
                link(pool.affine_select(out=m, in_=m, compare_op=op, fill=0.0, base=base,
                                        pattern=[[-1, P]], channel_multiplier=1))

            link(pool.memset(ident[:, :], 0.0))
            link(pool.affine_select(out=ident[:, :], in_=ident[:, :], compare_op=ALU.not_equal,
                                    fill=1.0, base=0, pattern=[[-1, P]], channel_multiplier=1))
            row = KT
            for src, k in par_src:
                if k == 32:
                    src = src.rearrange("w (b p) -> (w b) p", p=P)
                else:
                    src = src.rearrange("(b p) -> b p", p=P)
                pool.dma_start(rows[row:row + k, :], src).then_inc(par_in, 16)
                row += k
            pool.memset(neg_half[:, :], -0.5).then_inc(consts, 1)
            link(pool.memset(gate_w[:, :, :].bitcast(F32), 0.0))
            link(pool.memset(w_up_gate, 0.0))
            pool.dma_start(w_up_gate[0:RANK, :], gla_w_gate_up[0]).then_inc(up_in, 16)
            pool.dma_start(w_up_gate[32:32 + RANK, :], gla_w_gate_up[0]).then_inc(up_in, 16)
            pool.dma_start(b_gate, gla_b_gate[0].partition_broadcast(P)).then_inc(up_in, 16)
            pool.memset(spans[:, :, :], 0.0).then_inc(consts, 1)
            triangle(suffix[:, :], 1.0 / 16, ALU.is_gt)
            link(pool.affine_select(out=suffix[:, 0:CHUNK], in_=suffix[:, 0:CHUNK],
                                    compare_op=ALU.is_ge, fill=0.0, base=CHUNK - 1,
                                    pattern=[[0, CHUNK]], channel_multiplier=-1))
            for t, p0, a, b in ((0, 64, 0, 1), (1, 64, 2, 3), (1, 0, 5, 7), (1, 64, 6, 7)):
                link(pool.memset(spans[p0:p0 + 64, t, a:b], 1.0 / 16))
            triangle(draft[:, 0, :], -1.0, ALU.is_ge)
            triangle(draft[:, 1, :], -2.0 ** 100, ALU.is_ge)
            pool.tensor_copy(ident_r[:, :], ident[:, :])
            pool.tensor_copy(below[:, :], draft[:, 0, :])
            pool.tensor_copy(neg_mask[:, :], draft[:, 1, :])
            pool.memset(neg_ones[:, :].bitcast(F32), -1.0).then_inc(consts, 1)
            pool.dma_start(qk_gain[:, 0:1], q_norm_gain_2[0].rearrange("(p a) -> p a", a=1)).then_inc(gain_in, 16)
            pool.dma_start(qk_gain[:, 1:2], k_norm_gain_2[0].rearrange("(p a) -> p a", a=1)).then_inc(gain_in, 16)
            pool.dma_start(o_gain[:, :], gla_o_norm[0].partition_broadcast(P)).then_inc(gain_in, 16)

            def power(i):
                pool.wait_ge(ms_ready, i + 1)
                w = ST_WIDTH[i]
                pool.tensor_tensor(rs[:, i, 0:w], ms[:, i, 0:w], neg_half[:, 0:w], ALU.pow)\
                    .then_inc(rs_ready, 1)

            pool.wait_ge(consts, 3)
            for i in range(ST_MLP):
                power(i)
            pool.wait_ge(chunk_used, CH * (FIRST_O + 1))
            pool.wait_ge(tp_lo, groups_before(FIRST_O + 1))
            pool.dma_start(fin_gain, final_norm.partition_broadcast(P)).then_inc(late_in, 16)
            pool.dma_start(lru_w[:, 0, :, :], lru_w_a_2[0].rearrange("g i j -> i g j")).then_inc(late_in, 16)
            pool.dma_start(lru_w[:, 1, :, :], lru_w_x_2[0].rearrange("g i j -> i g j")).then_inc(late_in, 16)
            for i in range(ST_MLP, ST_ALL):
                power(i)

        @block.tensor
        def _(pe):
            def operand(kind):
                return (xa_hi, xa_lo) if kind in "kqvruxKQVgl" else (xb_hi, xb_lo)

            def multiply(t, c, it):
                n = CH * t + c
                xh, xl = operand(KINDS[t])
                if c == 0:
                    if t >= 2:
                        for s, kinds in ((acc_read_act, "kqvruxKQVgl"), (acc_read_dve, "kqvouDdxKQVf")):
                            pe.wait_ge(s, at(lambda q: count(kinds, q - 2), t, it))
                first = KINDS[t] != KINDS[t - 1] and KINDS[t] in "oudDxf" or t == 0
                if first:
                    if t == 0:
                        pe.wait_ge(tp_lo, c + 1)
                    else:
                        src = {"o": lambda q: FIRST_O - 8 + 1 + 2 * (c // 2),
                               "u": lambda q: (q if q == FIRST_U else FIRST_U) - 4 + c // 2,
                               "d": lambda q: q - 4 + c // 2, "D": lambda q: q - 4 + c // 2,
                               "x": lambda q: q - 4 + c // 2, "f": lambda q: q - 4 + c // 2}[KINDS[t]]
                        pe.wait_ge(tp_lo, at(lambda q: groups_before(src(q) + 1) + c % 2 + 1, t, it))
                pe.wait_ge(lo_ready, at(lambda q: CH * q + c + 1, t, it))
                for k in range(CK):
                    kt = CK * c + k
                    for tt in range(TT):
                        o = acc[:, t % 2, tt, :]
                        xs = slice(tt * P, (tt + 1) * P)
                        pe.matmul(o, xh[:, kt, xs], w_hi[:, n % RING, k, :], start=kt == 0, stop=False)
                        pe.matmul(o, xh[:, kt, xs], w_lo[:, n % RING, k, :], start=False, stop=False)
                        last = pe.matmul(o, xl[:, kt, xs], w_hi[:, n % RING, k, :], start=False,
                                         stop=kt == KT - 1)
                last.then_inc(chunk_used, 1)

            def multiply_first():
                pe.wait_ge(hi_ready, 1)
                pe.wait_ge(tp_hi, 1)
                for xs, ws in ((xa_hi, w_hi), (xa_hi, w_lo), (xa_lo, w_hi)):
                    if ws is w_lo:
                        pe.wait_ge(lo_ready, 1)
                    if xs is xa_lo:
                        pe.wait_ge(tp_lo, 1)
                    for kt in range(CK):
                        for tt in range(TT):
                            last = pe.matmul(acc[:, 0, tt, :], xs[:, kt, tt * P:(tt + 1) * P],
                                             ws[:, 0, kt, :], start=ws is w_hi and xs is xa_hi and kt == 0,
                                             stop=False)
                last.then_inc(chunk_used, 1)

            def group(g, it_wait, src):
                if it_wait is not None:
                    pe.wait_ge(tp_hi, it_wait)
                    pe.wait_ge(tp_lo, it_wait)
                for k in range(2):
                    for tt in range(TT):
                        last = pe.transpose(tp[:, g % 2, (2 * k + tt) * P:(2 * k + tt + 1) * P],
                                            src(k, tt), ident[:, :])
                last.then_inc(tp_ready, 1)

            def turn_panel(t, it):
                q = t - 1
                kind = KINDS[q]
                if kind in "qx":
                    pe.wait_ge(stage_act, at(lambda u: count("quxKQ", u - 1), t, it))
                if kind == "o":
                    pe.wait_ge(h_added, count("odD", q))
                else:
                    pe.wait_ge(stage_dve, at(lambda u: count("qruDxKQgl", u - 1), t, it))
                for g in range(2):
                    def src(k, tt):
                        f = 2 * g + k
                        if kind in "oD":
                            j = (q - KINDS.index(kind)) * 4 + f
                            return h[:, tt, j * P:(j + 1) * P]
                        return stage[:, q % 2, tt, f * P:(f + 1) * P]
                    group(g, at(lambda u: groups_before(u) + g - 1, t, it), src)

            def turn_x(g):
                if g % 2 == 0:
                    pe.wait_ge(x_in[g // 2], 16)
                group(g, g - 1 if g >= 2 else None,
                      lambda k, tt: h[:, tt, (2 * g + k) * P:(2 * g + k + 1) * P])

            def gate_low():
                pe.wait_ge(wg_lo, 1)
                pe.wait_ge(tp_lo, CH)
                for kt in range(KT):
                    for i, xs in enumerate((xa_hi, xa_lo)):
                        last = pe.matmul(aux[:, 0, 0:S], gate_w[:, kt, :], xs[:, kt, :],
                                         start=kt == 0 and i == 0, stop=kt == KT - 1 and i == 1)
                last.then_inc(low_ready, 1)

            def gate_up(i):
                tt, half = divmod(i, 2)
                pe.wait_ge(low_out, 1)
                if i >= 2:
                    pe.wait_ge(gate_out, i - 1)
                else:
                    pe.wait_ge(up_in, 48)
                pe.matmul(aux[:, (i + 1) % 2, :], g_low[:, tt * P:(tt + 1) * P],
                          w_up_gate[:, half * N:(half + 1) * N], start=True, stop=True)\
                    .then_inc(gate_ready, 1)

            def span_sums():
                pe.wait_ge(log_ready, 2)
                for k in range(8):
                    for tt in range(TT):
                        last = pe.matmul(aux[:, 0, k * 7:(k + 1) * 7], log_a[:, tt, k * P:(k + 1) * P],
                                         spans[:, tt, :], start=tt == 0, stop=tt == 1)
                last.then_inc(span_ready, 1)

            def suffix_sums(i):
                tt, half = divmod(i, 2)
                if i == 0:
                    pe.wait_ge(gate_out, 4)
                if i == 1:
                    pe.wait_ge(decay_ready, 1)
                if i >= 2:
                    pe.wait_ge(suf_out, i - 1)
                pe.matmul(aux[:, (i + 1) % 2, :], suffix[:, :], log_a[:, tt, half * N:(half + 1) * N],
                          start=True, stop=True).then_inc(suf_ready, 1)

            def turn_keys(g):
                g0 = groups_before(2)
                if g == 0:
                    pe.wait_ge(keys_ready, 2)
                group(g, g0 + g - 1, lambda k, tt: keys[:, tt, (2 * g + k) * P:(2 * g + k + 1) * P])

            def gla_scores(hd):
                pe.wait_ge(sq_q, hd + 1)
                pe.wait_ge(tp_hi, groups_before(3))
                if hd >= 2:
                    pe.wait_ge(sc_act, hd - 1)
                    pe.wait_ge(sc_dve, hd - 1)
                b = aux[:, hd % 2, :].rearrange("p (s t) -> p s t", s=TT)
                for k in range(2):
                    kk = 2 * hd + k
                    pe.matmul(b[:, 0, CHUNK:], key_s[:, kk, 0:P], far_q[:, hd % 2, k, :],
                              start=k == 0, stop=k == 1)
                for st in range(TT):
                    for k in range(2):
                        kk = 2 * hd + k
                        own = slice(st * P, st * P + CHUNK)
                        pe.matmul(b[0:CHUNK, st, own], key_t[:, kk, own], qry_t[:, kk, own],
                                  start=k == 0, stop=k == 1)
                for k in range(2):
                    kk = 2 * hd + k
                    last = pe.matmul(b[:, 1, S - CHUNK:], key_s[:, kk, P:S], qry_t[:, kk, S - CHUNK:],
                                     start=k == 0, stop=k == 1)
                last.then_inc(sc_ready, 1)

            def gla_out(hd):
                pe.wait_ge(vals_act, hd + 1)
                pe.wait_ge(vals_dve, hd + 1)
                if hd == 0:
                    pe.wait_ge(sc_act, GH)
                    pe.wait_ge(sc_dve, GH)
                else:
                    pe.wait_ge(o_read, hd)
                pe.matmul(aux[:, 0, :], scores[:, hd, 0:P], vals[:, 0, :], start=True, stop=True)
                pe.matmul(aux[:, 1, :], scores[:, hd, P:2 * P], vals[:, 0, :], start=True, stop=False)
                pe.matmul(aux[:, 1, :], scores[:, hd, 2 * P:3 * P], vals[:, 1, :], start=False, stop=True)\
                    .then_inc(o_ready, 1)

            def lru_gates(b):
                pe.wait_ge(conv_ready, b // 4 + 1)
                if b >= 2:
                    pe.wait_ge(lru_th, b - 1)
                else:
                    pe.wait_ge(late_in, 48)
                for i in range(2):
                    last = pe.matmul(aux[:, b % 2, i * S:(i + 1) * S], lru_w[:, i, b, :],
                                     conv[:, b % 4, :], start=i == 0, stop=True, skip_group_check=True)
                last.then_inc(lru_mm, 1)

            def sb_logits(hd):
                if hd == 0:
                    pe.wait_ge(tp_hi, groups_before(ATTEND))
                    pe.wait_ge(tp_lo, groups_before(ATTEND))
                if hd >= 2:
                    pe.wait_ge(y_out, hd - 1)
                b = aux[:, hd % 2, :]
                pe.matmul(b[:, 0:S], k2_t[:, hd, 0:P], q2_t[:, hd, :], start=True, stop=False,
                          skip_group_check=True)
                pe.matmul(b[:, S:S + P], k2_t[:, hd, P:S], q2_t[:, hd, P:S], start=False, stop=False,
                          skip_group_check=True)
                pe.matmul(b[:, 0:P], ident_r[:, :], neg_mask[:, :], start=False, stop=False,
                          skip_group_check=True)
                pe.matmul(b[:, S:S + P], ident_r[:, :], neg_mask[:, :], start=False, stop=False,
                          skip_group_check=True).then_inc(z_ready, 1)

            def sb_breaks(hd):
                pe.wait_ge(sp_out, hd + 1)
                b = aux[:, hd % 2, :]
                for part in (sp_hi, sp_lo):
                    pe.matmul(b[:, 0:384], below[:, :], part[:, hd % 2, :], start=False, stop=False,
                              skip_group_check=True)
                for part in (sp_hi, sp_lo):
                    last = pe.matmul(b[:, P:S], neg_ones[:, :], part[:, hd % 2, S:S + P], start=False,
                                     stop=part is sp_lo, skip_group_check=True)
                last.then_inc(lw_ready, 1)

            def sb_values(hd):
                pe.wait_ge(w_out_s, hd + 1)
                pe.wait_ge(v2_act, hd // 4 + 1)
                pe.wait_ge(v2_dve, hd // 4 + 1)
                b = aux[:, hd % 2, :]
                w = wts[:, hd % 2, :]
                v = slice(hd * P, (hd + 1) * P)
                pe.matmul(b[:, 0:S], v2[:, 0, v], w[:, 0:S], start=True, stop=False, skip_group_check=True)
                pe.matmul(b[:, P:S], v2[:, 1, v], w[:, S:S + P], start=False, stop=True,
                          skip_group_check=True).then_inc(y_ready, 1)

            def after(t, c, it):
                prev = KINDS[t - 1] if t else ""
                late = 6 if prev in "KQ" else 3 if prev == "D" or prev == "r" and t < FIRST_O else 2
                if t >= 1 and prev in "qroguDxlKQ" and c == late:
                    turn_panel(t, it)
                if t == 0:
                    if c == 0:
                        turn_x(2)
                        turn_x(3)
                    if 1 <= c <= 4:
                        turn_x(c + 3)
                    if c == 4:
                        pe.wait_ge(par_in, 16 * len(par_src))
                        pe.wait_ge(par_ready, 1)
                        pe.transpose(aux[:, 1, 0:P], rows[:, :], ident[:, :]).then_inc(par_turned, 1)
                    if c == 6:
                        gate_low()
                    if c == 7:
                        pe.wait_ge(par_ready, 2)
                        gate_up(0)
                        gate_up(1)
                if t == 1:
                    if c == 1:
                        gate_up(2)
                        gate_up(3)
                    if c == 7:
                        span_sums()
                if t == 2:
                    if c == 0:
                        suffix_sums(0)
                        suffix_sums(1)
                    if c == 2:
                        suffix_sums(2)
                        suffix_sums(3)
                    if c in (5, 7):
                        turn_keys(c - 5)
                        turn_keys(c - 4)
                if t in (3, 4) and c in (5, 7):
                    gla_scores((t - 3) * 2 + (c - 5) // 2)
                if prev == "v" and c == 2:
                    gla_out((t - 1 - FIRST_V) // 2)
                for j in range(2):
                    step = lru_step(t, c, j)
                    if step in (0, 1):
                        lru_gates(4 * j + 2 * step)
                        lru_gates(4 * j + 2 * step + 1)
                if ATTEND <= t < ATTEND_END and c < 6:
                    (sb_logits, sb_breaks, sb_values)[c // 2](2 * (t - ATTEND) + c % 2)

            def run(t, it=None):
                for c in range(CH):
                    if t == 0 and c == 0:
                        multiply_first()
                    else:
                        multiply(t, c, it)
                    after(t, c, it)

            pe.wait_ge(pool_chain, 2)
            pe.wait_ge(norm_in, 16)
            pe.transpose(aux[:, 1, 0:KT], rows[0:KT, :], ident[0:KT, 0:KT]).then_inc(par_turned, 1)
            turn_x(0)
            turn_x(1)
            for t in range(FIRST_U + 1):
                run(t)
            with pe.Fori(0, MLP_BLOCKS - 1) as it:
                for t in range(FIRST_U + 1, FIRST_U + 1 + BODY):
                    run(t, it)
            for t in range(FIRST_U + 1 + BODY * (MLP_BLOCKS - 1), PANELS):
                run(t)

        def panel_done(eng, t, it):
            eng.wait_ge(chunk_used, at(lambda q: CH * q, t, it))

        @block.scalar
        def _(act):
            steps = [0]

            def link(ins):
                steps[0] += 1
                ins.then_inc(act_chain, 1)
                act.wait_ge(act_chain, steps[0])

            def split_hi(t, c, it):
                n = CH * t + RING + c
                if n >= CH * PANELS:
                    return
                act.wait_ge(raw_in[n % RING], at(lambda q: 16 * ((CH * q + RING + c) // RING + 1), t, it))
                act.wait_ge(chunk_used, at(lambda q: CH * q + c + 1, t, it))
                act.activation(w_hi[:, n % RING, :, :], raw[:, n % RING, :, :], ACT.Copy)\
                    .then_inc(hi_ready, 1)

            def split_x(bank, dst, k0, gain, wait):
                act.wait_ge(tp_ready, wait)
                if gain is None:
                    act.activation(dst[:, k0:k0 + 2, :].rearrange("p a b -> p (a b)"), tp[:, bank, :],
                                   ACT.Copy).then_inc(tp_hi, 1)
                    return
                for k in range(2):
                    ins = act.activation(dst[:, k0 + k, :], tp[:, bank, k * S:(k + 1) * S], ACT.Copy,
                                         scale=par[:, gain + k0 + k:gain + k0 + k + 1])
                ins.then_inc(tp_hi, 1)

            def move_first(dst, done, scale=1.0):
                act.wait_ge(tp_ready, done)
                act.activation(dst, tp[:, 0, :].rearrange("p (a b) -> p a b", b=S), ACT.Copy,
                               scale=scale).then_inc(tp_hi, 1)
                act.wait_ge(tp_hi, done)
                act.sem_inc(tp_hi, 1)

            def squares(src, col, junk_to):
                act.activation(junk_to, src, ACT.Square, accum_out=sums[:, col:col + 1])\
                    .then_inc(sq_ready, 1)
                sq_count[0] += 1
                act.wait_ge(sq_ready, sq_count[0])

            sq_count = [0]

            def before(t, c, it):
                prev = KINDS[t - 1] if t else ""
                q = t - 1
                b = q % 2
                if c == 0 and t:
                    if prev == "k":
                        if q == 0:
                            act.wait_ge(r1_ready, 1)
                        panel_done(act, t, it)
                        act.activation(keys[:, 0, q * N:(q + 1) * N], acc[:, b, 0, :], ACT.Copy,
                                       scale=rs[:, ST_X, 0:1]).then_inc(acc_read_act, 1)
                    if prev == "q":
                        panel_done(act, t, it)
                        act.activation(stage[:, b, 0, :], acc[:, b, 0, :], ACT.Copy,
                                       scale=scl[:, R1S:R1S + 1]).then_inc(acc_read_act, 1)
                        act.wait_ge(acc_read_act, count("kqvruxKQVgl", q))
                        act.sem_inc(stage_act, 1)
                    if prev == "v":
                        hd = (t - 1 - FIRST_V) // 2
                        panel_done(act, t, it)
                        if hd == 0:
                            act.wait_ge(tp_hi, groups_before(3))
                        act.activation(vals[:, 0, :], acc[:, b, 0, :], ACT.Copy, scale=rs[:, ST_X, 0:1])\
                            .then_inc(acc_read_act, 1)
                        act.wait_ge(acc_read_act, count("kqvruxKQVgl", q))
                        act.sem_inc(vals_act, 1)
                    if prev in "rgl":
                        panel_done(act, t, it)
                        half = scl[:, R1H:R1H + 2] if prev == "r" else scl[:, R2H:R2H + 2]
                        tanh_to = th if prev == "r" else stage[:, b, :, :]
                        z_to = zt if prev == "r" else zt2
                        n_silu = count("rgl", q)
                        if n_silu > 1:
                            act.wait_ge(stage_dve, count("qruDxKQgl", q) - 1)
                        for tt in range(TT):
                            act.activation(z_to[:, tt, :], acc[:, b, tt, :], ACT.Copy,
                                           scale=half[:, tt:tt + 1])
                            last = act.activation(tanh_to[:, tt, :], acc[:, b, tt, :], ACT.Tanh,
                                                  scale=half[:, tt:tt + 1])
                        last.then_inc(silu_act, 1)
                        act.wait_ge(silu_act, n_silu)
                        act.sem_inc(acc_read_act, 1)
                    if prev == "u":
                        panel_done(act, t, it)
                        act.wait_ge(rs_ready, ST_MLP + 1)
                        act.activation(stage[:, b, 0, :], acc[:, b, 0, :], ACT.Relu,
                                       scale=rs[:, ST_MLP, 0:1]).then_inc(acc_read_act, 1)
                        act.wait_ge(acc_read_act, at(lambda u: count("kqvruxKQVgl", u - 1), t, it))
                        act.sem_inc(stage_act, 1)
                    if prev in "xKQ":
                        if q == FIRST_X:
                            act.wait_ge(r2_ready, 1)
                        panel_done(act, t, it)
                        act.activation(stage[:, b, 0, :], acc[:, b, 0, :], ACT.Copy,
                                       scale=scl[:, R2:R2 + 1]).then_inc(acc_read_act, 1)
                        act.wait_ge(acc_read_act, count("kqvruxKQVgl", q))
                        act.sem_inc(stage_act, 1)
                    if prev == "V":
                        j = q - FIRST_V2
                        panel_done(act, t, it)
                        act.activation(v2[:, 0, j * N:(j + 1) * N], acc[:, b, 0, :], ACT.Copy,
                                       scale=scl[:, R2:R2 + 1]).then_inc(acc_read_act, 1)
                        act.wait_ge(acc_read_act, count("kqvruxKQVgl", q))
                        act.sem_inc(v2_act, 1)
                if prev == "o" and c == 1:
                    j = q - FIRST_O
                    act.wait_ge(h_added, count("odD", q))
                    for tt in range(TT):
                        squares(h[:, tt, j * N:(j + 1) * N], Q_M + 4 * tt + j, junk_h)
                if prev == "D" and c == 0:
                    j = q - FIRST_DL
                    act.wait_ge(h_added, count("odD", q))
                    for tt in range(TT):
                        squares(h[:, tt, j * N:(j + 1) * N], Q_F + 4 * tt + j, junk_h)
                    act.sem_inc(h_squared, 1)
                if prev == "D" and c == 3:
                    j = q - FIRST_DL
                    act.wait_ge(stage_dve, count("qruDxKQgl", q))
                    for tt in range(TT):
                        squares(h[:, tt, j * N:(j + 1) * N], Q_N + 4 * tt + j, junk_h)
                if prev and prev in "qrouDx" and c == (4 if prev == "D" or prev == "r" and t < FIRST_O else 3):
                    for g in range(2):
                        G = at(lambda u: groups_before(u) + g + 1, t, it)
                        if prev == "q" and g == 0:
                            move_first(qry_t[:, 4 * (q - FIRST_Q):4 * (q - FIRST_Q) + 2, :], G)
                        if prev == "r":
                            split_x(g, xb_hi, 4 * ((t - 1 - FIRST_R) // 2) + 2 * g, None, G)
                        if prev == "o":
                            split_x(g, xa_hi, 4 * (q - FIRST_O) + 2 * g, C_MLP, G)
                        if prev == "u":
                            split_x(g, xb_hi, 4 * ((q - FIRST_U) % 4) + 2 * g, None, G)
                        if prev == "D":
                            split_x(g, xa_hi, 4 * (q - FIRST_DL) + 2 * g, C_N2, G)
                        if prev == "x" and g == 0:
                            if q == FIRST_X + 1:
                                act.wait_ge(conv_ready, 1)
                            move_first(lru_x[:, 0:2, PAD:PAD + S], G)
                if prev and prev in "gl" and c == (7 if q == FIRST_G + 1 else 3):
                    for g in range(2):
                        k = 4 * (q - FIRST_G) + 2 * g
                        act.wait_ge(prod_out, 2 * (q - FIRST_G) + g + 1)
                        act.activation(xb_hi[:, k:k + 2, :].rearrange("p a b -> p (a b)"),
                                       prod[:, g, :], ACT.Copy).then_inc(tp_hi, 1)
                if c == 7 and prev and prev in "KQ":
                    k = 4 * ((q - FIRST_K2) % 2)
                    if prev == "K":
                        move_first(k2_t[:, k:k + 2, :], groups_before(t) + 1)
                    else:
                        move_first(q2_t[:, k:k + 2, :], groups_before(t) + 1, qk_gain[:, 2:3])
                if t == 0:
                    if 2 <= c <= 5:
                        g = c + 2
                        split_x(g % 2, xa_hi, 2 * g, C_GLA, g + 1)
                    if c == 3:
                        act.wait_ge(wg_in, 16)
                        act.wait_ge(pool_chain, 3)
                        act.activation(gate_w[:, :, 0:RANK], wg_raw, ACT.Copy).then_inc(wg_hi, 1)
                    if c in (5, 6):
                        squares(h[:, c - 5, :], Q_X + c - 5, junk)
                if t == 1:
                    if c in (2, 4):
                        if c == 2:
                            act.preload_act_table_set("natural_log_exp_and_others")
                        tt = (c - 2) // 2
                        act.wait_ge(gate_out, 2 * tt + 2)
                        z = z_gate[:, 2 * tt:2 * tt + 2, :].rearrange("p a b -> p (a b)")
                        link(act.activation(log_a[:, tt, :], z, ACT.Abs))
                        link(act.activation(log_a[:, tt, :], log_a[:, tt, :], ACT.Exp, scale=-1.0))
                        act.activation(log_a[:, tt, :], log_a[:, tt, :], ACT.Ln, bias=1.0)\
                            .then_inc(ln_ready, 1)
                    if c == 5:
                        act.wait_ge(par_ready, 2)
                        t0 = lru_par[:, L_T:L_T + 8]
                        link(act.activation(t0, par[:, C_LAM:C_LAM + 8], ACT.Abs))
                        link(act.activation(t0, t0, ACT.Exp, scale=-1.0))
                        act.activation(t0, t0, ACT.Ln, bias=1.0).then_inc(lam_act, 1)
                    if c == 7:
                        act.wait_ge(span_ready, 1)
                        act.activation(decay.rearrange("p a b -> p (a b)"), aux[:, 0, 0:8 * 7], ACT.Exp)\
                            .then_inc(decay_ready, 1)
                if t == 2:
                    if c in (1, 3):
                        for i in (c - 1, c):
                            tt, half = divmod(i, 2)
                            act.wait_ge(suf_ready, i + 1)
                            act.activation(log_a[:, tt, half * N:(half + 1) * N], aux[:, (i + 1) % 2, :],
                                           ACT.Exp).then_inc(suf_out, 1)
                    if c == 6:
                        move_first(key_t[:, 0:2, :], groups_before(2) + 1)
                if t == 3 and c == 1:
                    move_first(key_t[:, 4:6, :], groups_before(2) + 3)
                if (t, c) in SCORES_OUT:
                    hd = SCORES_OUT.index((t, c))
                    act.wait_ge(sc_ready, hd + 1)
                    act.activation(scores[0:64, hd, 0:S], aux[0:64, hd % 2, 0:S], ACT.Copy)
                    act.activation(scores[0:64, hd, S:S + P], aux[0:64, hd % 2, S + P:2 * S], ACT.Copy)\
                        .then_inc(sc_act, 1)
                if prev == "v" and c == 3:
                    hd = (t - 1 - FIRST_V) // 2
                    act.wait_ge(o_ready, hd + 1)
                    for tt in range(TT):
                        squares(aux[:, tt, :], Q_O + 2 * hd + tt, junk_o)
                for j in range(2):
                    step = lru_step(t, c, j)
                    for i in range(2 if step in (1, 2) else 0):
                        blk = 4 * j + 2 * (step - 1) + i
                        act.wait_ge(lru_mm, blk + 1)
                        if blk == 4:
                            act.wait_ge(lru_done, 1)
                        if blk == 0:
                            act.wait_ge(lam_ready, 1)
                        act.activation(th_r[:, blk % 4, :], aux[:, blk % 2, 0:S], ACT.Tanh,
                                       bias=lru_par[:, L_BA + blk:L_BA + blk + 1], scale=0.5)
                        act.activation(th_i[:, blk % 4, :], aux[:, blk % 2, S:2 * S], ACT.Tanh,
                                       bias=lru_par[:, L_BX + blk:L_BX + blk + 1], scale=0.5)\
                            .then_inc(lru_th, 1)
                for j in range(2):
                    step = lru_step(t, c, j)
                    if step == 3:
                        act.wait_ge(lru_th, 4 * j + 4)
                        for i in range(4):
                            col = 4 * j + i
                            sp4 = lru_par[:, L_SP + col:L_SP + col + 1]
                            neg4 = lru_par[:, L_NEG + col:L_NEG + col + 1]
                            act.activation(lru_a[:, i, :], th_r[:, i, :], ACT.Exp, bias=neg4, scale=neg4)
                            last = act.activation(lru_u[:, i, :], th_r[:, i, :], ACT.Tanh, bias=sp4, scale=sp4)
                        last.then_inc(lru_exp, 1)
                    if step == 5:
                        act.wait_ge(lru_sq, j + 1)
                        act.activation(lru_u, lru_u, ACT.Sqrt, scale=0.25).then_inc(lru_root, 1)
                if prev and prev in "KQ" and c == 1:
                    act.wait_ge(kq_sq, q - FIRST_K2 + 1)
                    act.activation(sq2, stage[:, b, :, :], ACT.Square).then_inc(kq_red, 1)
                if ATTEND <= t < ATTEND_END:
                    if c == 1:
                        act.preload_act_table_set("natural_log_exp_and_others")
                    if c in (1, 2):
                        hd = 2 * (t - ATTEND) + c - 1
                        act.wait_ge(z_ready, hd + 1)
                        e = soft[:, hd % 2, :]
                        link(act.activation(e, aux[:, hd % 2, 0:384], ACT.Abs))
                        link(act.activation(e, e, ACT.Exp, scale=-1.0))
                        act.activation(e, e, ACT.Ln, bias=1.0).then_inc(ln_out, 1)
                    if c in (3, 4):
                        hd = 2 * (t - ATTEND) + c - 3
                        act.wait_ge(lw_ready, hd + 1)
                        act.activation(wts[:, hd % 2, :], aux[:, hd % 2, 0:384], ACT.Exp)\
                            .then_inc(w_out_s, 1)

            def run(t, it=None):
                for c in range(CH):
                    before(t, c, it)
                    if t < PANELS:
                        split_hi(t, c, it)

            for j in range(2):
                act.dma_start(h[:, :, j * N:(j + 1) * N], x_v[:, :, j * N:(j + 1) * N])\
                    .then_inc(x_in[j], 16)
            act.wait_ge(raw_in[0], 16)
            act.activation(w_hi[:, 0, :, :], raw[:, 0, :, :], ACT.Copy).then_inc(hi_ready, 1)
            act.wait_ge(par_ready, 1)
            split_x(0, xa_hi, 0, C_GLA, 1)
            for n in range(1, RING):
                split_x(n % 2, xa_hi, 2 * n, C_GLA, n + 1)
                act.wait_ge(raw_in[n], 16)
                act.activation(w_hi[:, n, :, :], raw[:, n, :, :], ACT.Copy).then_inc(hi_ready, 1)
            for t in range(FIRST_U + 1):
                run(t)
            with act.Fori(0, MLP_BLOCKS - 1) as it:
                for t in range(FIRST_U + 1, FIRST_U + 1 + BODY):
                    run(t, it)
            for t in range(FIRST_U + 1 + BODY * (MLP_BLOCKS - 1), PANELS + 1):
                run(t)

        @block.vector
        def _(dve):
            steps = [0]

            def link(ins):
                steps[0] += 1
                ins.then_inc(dve_chain, 1)
                dve.wait_ge(dve_chain, steps[0])

            def split_lo(t, c, it):
                n = CH * t + RING + c
                if n >= CH * PANELS:
                    return
                dve.wait_ge(hi_ready, at(lambda q: CH * q + RING + c + 1, t, it))
                dve.tensor_tensor(w_lo[:, n % RING, :, :], raw[:, n % RING, :, :],
                                  w_hi[:, n % RING, :, :].bitcast(F32), ALU.subtract).then_inc(lo_ready, 1)

            def rest_x(bank, hi, lo, k0, gain, wait):
                dve.wait_ge(tp_hi, wait)
                if gain is None:
                    dve.tensor_tensor(lo[:, k0:k0 + 2, :].rearrange("p a b -> p (a b)"), tp[:, bank, :],
                                      hi[:, k0:k0 + 2, :].rearrange("p a b -> p (a b)").bitcast(F32),
                                      ALU.subtract).then_inc(tp_lo, 1)
                    return
                for k in range(2):
                    ins = dve.scalar_tensor_tensor(
                        out=lo[:, k0 + k, :], in0=tp[:, bank, k * S:(k + 1) * S],
                        scalar=par[:, gain + k0 + k:gain + k0 + k + 1],
                        in1=hi[:, k0 + k, :].bitcast(F32), op0=ALU.mult, op1=ALU.subtract)
                ins.then_inc(tp_lo, 1)

            def move_second(dst, done, scale=None):
                dve.wait_ge(tp_lo, done - 2)
                dve.sem_inc(tp_lo, 1)
                dve.wait_ge(tp_ready, done)
                src = tp[:, 1, :].rearrange("p (a b) -> p a b", b=S)
                if scale is None:
                    dve.tensor_copy(dst, src).then_inc(tp_lo, 1)
                else:
                    dve.tensor_scalar(dst, src, scale, None, ALU.mult).then_inc(tp_lo, 1)

            def mean(i, src, width):
                dve.tensor_scalar(ms[:, i, 0:ST_WIDTH[i]], src, 1.0 / width, EPS, ALU.mult, ALU.add)\
                    .then_inc(ms_ready, 1)

            def half_panel(t, it, dst, scale):
                panel_done(dve, t, it)
                dve.tensor_scalar(dst, acc[:, (t - 1) % 2, 1, :], scale, None, ALU.mult)\
                    .then_inc(acc_read_dve, 1)
                dve.wait_ge(acc_read_dve, count("kqvouDdxKQVf", t - 1))

            def decay_head(hd):
                if hd >= 2:
                    dve.wait_ge(sc_ready, hd - 1)
                if hd % 2 == 0:
                    dve.wait_ge(tp_hi, groups_before(4 + hd // 2))
                    dve.wait_ge(tp_lo, groups_before(4 + hd // 2))
                ks = slice(2 * hd, 2 * hd + 2)
                for out_, in_, d, n in (
                        (key_s[:, ks, :], key_t[:, ks, :], decay[:, ks, 0:4], 4),
                        (far_q[:, hd % 2, :, :], qry_t[:, ks, CHUNK:], decay[:, ks, 4:7], 3)):
                    ins = dve.tensor_tensor(
                        out_.rearrange("p k (n s) -> p k n s", n=n),
                        in_.rearrange("p k (n s) -> p k n s", n=n),
                        d.unsqueeze(3).to_broadcast([P, 2, n, CHUNK]), ALU.mult)
                ins.then_inc(sq_q, 1)

            def before(t, c, it):
                prev = KINDS[t - 1] if t else ""
                q = t - 1
                b = q % 2
                if c == 0 and t:
                    if prev == "k":
                        if q == 0:
                            dve.wait_ge(rs_ready, 1)
                        half_panel(t, it, keys[:, 1, q * N:(q + 1) * N], rs[:, ST_X, 1:2])
                    if prev == "q":
                        half_panel(t, it, stage[:, b, 1, :], scl[:, R1S + 1:R1S + 2])
                        dve.sem_inc(stage_dve, 1)
                    if prev == "v":
                        if q == 4:
                            dve.wait_ge(tp_hi, groups_before(3))
                        half_panel(t, it, vals[:, 1, :], rs[:, ST_X, 1:2])
                        dve.sem_inc(vals_dve, 1)
                    if prev == "r":
                        hd = (t - 1 - FIRST_R) // 2
                        dve.wait_ge(silu_act, hd + 1)
                        if hd == 0:
                            dve.wait_ge(gain_in, 48)
                        link(dve.scalar_tensor_tensor(out=th, in0=th, scalar=1.0, in1=zt,
                                                      op0=ALU.add, op1=ALU.mult))
                        link(dve.tensor_tensor(th, th, o_gain[:, :].unsqueeze(1).to_broadcast([P, TT, N]),
                                               ALU.mult))
                        dve.wait_ge(rs_ready, ST_O + hd + 1)
                        for tt in range(TT):
                            ins = dve.scalar_tensor_tensor(
                                out=stage[:, b, tt, :], in0=aux[:, tt, :],
                                scalar=rs[:, ST_O + hd, tt:tt + 1], in1=th[:, tt, :],
                                op0=ALU.mult, op1=ALU.mult)
                        ins.then_inc(o_read, 1)
                        dve.wait_ge(o_read, hd + 1)
                        dve.sem_inc(stage_dve, 1)
                    if prev and prev in "odD":
                        j = (q - (FIRST_O if prev == "o" else FIRST_U + 4)) % 4
                        panel_done(dve, t, it)
                        prior = at(lambda u: count("odD", u - 1) - 4, t, it)
                        if prev != "o":
                            dve.wait_ge(h_added, prior)
                        if prev == "o" and j == 0:
                            dve.wait_ge(sq_ready, 2)
                        dve.tensor_tensor(h[:, :, j * N:(j + 1) * N], h[:, :, j * N:(j + 1) * N],
                                          acc[:, b, :, :], ALU.add).then_inc(h_added, 1)
                        dve.wait_ge(h_added, at(lambda u: count("odD", u - 1), t, it))
                        dve.sem_inc(acc_read_dve, 1)
                    if prev == "u":
                        panel_done(dve, t, it)
                        dve.wait_ge(rs_ready, ST_MLP + 1)
                        dve.tensor_scalar(stage[:, b, 1, :], acc[:, b, 1, :], rs[:, ST_MLP, 1:2], 0.0,
                                          ALU.mult, ALU.max).then_inc(acc_read_dve, 1)
                        dve.wait_ge(acc_read_dve, at(lambda u: count("kqvouDdxKQVf", u - 1), t, it))
                        dve.wait_ge(stage_act, at(lambda u: count("quxKQ", u - 1), t, it))
                        dve.tensor_tensor(stage[:, b, :, :], stage[:, b, :, :], stage[:, b, :, :],
                                          ALU.mult).then_inc(stage_dve, 1)
                    if prev in "xKQ":
                        if q == FIRST_X:
                            dve.wait_ge(r2_ready, 1)
                        half_panel(t, it, stage[:, b, 1, :], scl[:, R2 + 1:R2 + 2])
                        if prev == "x":
                            dve.sem_inc(stage_dve, 1)
                        else:
                            dve.wait_ge(stage_act, count("quxKQ", q))
                            dve.sem_inc(kq_sq, 1)
                    if prev == "V":
                        j = q - FIRST_V2
                        half_panel(t, it, v2[:, 1, j * N:(j + 1) * N], scl[:, R2 + 1:R2 + 2])
                        dve.sem_inc(v2_dve, 1)
                    if prev and prev in "gl":
                        dve.wait_ge(silu_act, count("rgl", q))
                        dve.scalar_tensor_tensor(out=stage[:, b, :, :], in0=stage[:, b, :, :], scalar=1.0,
                                                 in1=zt2, op0=ALU.add, op1=ALU.mult).then_inc(stage_dve, 1)
                    if prev == "f":
                        j = q - FIRST_F
                        panel_done(dve, t, it)
                        if j >= 2:
                            dve.wait_ge(out_sent[j % 2], 16 * TT)
                        for tt in range(TT):
                            dve.scalar_tensor_tensor(
                                out=stage[:, b, tt, :], in0=h[:, tt, j * N:(j + 1) * N],
                                scalar=rs[:, ST_FIN, tt:tt + 1], in1=acc[:, b, tt, :],
                                op0=ALU.mult, op1=ALU.add).then_inc(out_ready, 1)
                        dve.wait_ge(out_ready, TT * (j + 1))
                        dve.sem_inc(acc_read_dve, 1)
                if prev == "D" and c == 1:
                    j = q - FIRST_DL
                    if j == 0:
                        dve.wait_ge(late_in, 48)
                    dve.wait_ge(h_squared, j + 1)
                    dve.tensor_tensor(h[:, :, j * N:(j + 1) * N], h[:, :, j * N:(j + 1) * N],
                                      fin_gain[:, j * N:(j + 1) * N].unsqueeze(1).to_broadcast([P, TT, N]),
                                      ALU.mult).then_inc(stage_dve, 1)
                if prev and prev in "qrouDx" and c == (4 if prev == "D" or prev == "r" and t < FIRST_O else 3):
                    for g in range(2):
                        G = at(lambda u: groups_before(u) + g + 1, t, it)
                        if prev == "q" and g == 1:
                            move_second(qry_t[:, 4 * (q - FIRST_Q) + 2:4 * (q - FIRST_Q) + 4, :], G)
                        if prev == "r":
                            rest_x(g, xb_hi, xb_lo, 4 * ((t - 1 - FIRST_R) // 2) + 2 * g, None, G)
                        if prev == "o":
                            rest_x(g, xa_hi, xa_lo, 4 * (q - FIRST_O) + 2 * g, C_MLP, G)
                        if prev == "u":
                            rest_x(g, xb_hi, xb_lo, 4 * ((q - FIRST_U) % 4) + 2 * g, None, G)
                        if prev == "D":
                            rest_x(g, xa_hi, xa_lo, 4 * (q - FIRST_DL) + 2 * g, C_N2, G)
                        if prev == "x" and g == 1:
                            if q == FIRST_X:
                                link(dve.memset(lru_x[:, :, 0:PAD], 0.0))
                            move_second(lru_x[:, 2:4, PAD:PAD + S], G)
                if prev and prev in "gl" and c == (7 if q == FIRST_G + 1 else 3):
                    mixed = y_t if prev == "g" else lru_h
                    k0 = 4 * ((q - FIRST_G) % 2)
                    if prev == "g":
                        dve.wait_ge(y_out, k0 + 4)
                    else:
                        dve.wait_ge(lru_done, 2)
                    for g in range(2):
                        dve.wait_ge(tp_ready, groups_before(t) + g + 1)
                        if q > FIRST_G:
                            dve.wait_ge(tp_lo, groups_before(t))
                        dve.tensor_tensor(prod[:, g, :], tp[:, g, :],
                                          mixed[:, k0 + 2 * g:k0 + 2 * g + 2, :].rearrange("p a b -> p (a b)"),
                                          ALU.mult).then_inc(prod_out, 1)
                    for g in range(2):
                        k = 4 * (q - FIRST_G) + 2 * g
                        dve.wait_ge(tp_hi, groups_before(t) + g + 1)
                        dve.tensor_tensor(xb_lo[:, k:k + 2, :].rearrange("p a b -> p (a b)"), prod[:, g, :],
                                          xb_hi[:, k:k + 2, :].rearrange("p a b -> p (a b)").bitcast(F32),
                                          ALU.subtract).then_inc(tp_lo, 1)
                if c == 7 and prev and prev in "KQ":
                    k = 4 * ((q - FIRST_K2) % 2) + 2
                    if prev == "K":
                        move_second(k2_t[:, k:k + 2, :], groups_before(t) + 2)
                    else:
                        move_second(q2_t[:, k:k + 2, :], groups_before(t) + 2, qk_gain[:, 2:3])
                if t == FIRST_U and c == 2:
                    dve.wait_ge(sq_ready, 18)
                    link(dve.tensor_reduce(scl[:, T0:T0 + 2],
                                           sums[:, Q_M:Q_M + 8].rearrange("p (t j) -> p t j", j=4),
                                           AX.X, ALU.add))
                    mean(ST_MLP, scl[:, T0:T0 + 2], D)
                if t == FIRST_X and c == 4:
                    dve.wait_ge(sq_ready, 34)
                    link(dve.tensor_reduce(scl[:, T0:T0 + 2],
                                           sums[:, Q_F:Q_F + 8].rearrange("p (t j) -> p t j", j=4),
                                           AX.X, ALU.add))
                    mean(ST_FIN, scl[:, T0:T0 + 2], D)
                    link(dve.tensor_reduce(scl[:, T1:T1 + 2],
                                           sums[:, Q_N:Q_N + 8].rearrange("p (t j) -> p t j", j=4),
                                           AX.X, ALU.add))
                if t == FIRST_X and c == 6:
                    dve.wait_ge(rs_ready, ST_FIN + 1)
                    rf = rs[:, ST_FIN, 0:2]
                    link(dve.tensor_tensor(scl[:, RF2:RF2 + 2], rf, rf, ALU.mult))
                    link(dve.tensor_tensor(scl[:, T1:T1 + 2], scl[:, T1:T1 + 2], scl[:, RF2:RF2 + 2],
                                           ALU.mult))
                    mean(ST_N2, scl[:, T1:T1 + 2], D)
                if t == FIRST_X and c == 7:
                    dve.wait_ge(rs_ready, ST_N2 + 1)
                    link(dve.tensor_tensor(scl[:, R2:R2 + 2], rs[:, ST_FIN, 0:2], rs[:, ST_N2, 0:2],
                                           ALU.mult))
                    dve.tensor_scalar(scl[:, R2H:R2H + 2], scl[:, R2:R2 + 2], 0.5, None, ALU.mult)\
                        .then_inc(r2_ready, 1)
                if t == 0:
                    if 2 <= c <= 5:
                        g = c + 2
                        rest_x(g % 2, xa_hi, xa_lo, 2 * g, C_GLA, g + 1)
                    if c == 4:
                        dve.wait_ge(wg_hi, 1)
                        dve.tensor_tensor(gate_w[:, :, 32:32 + RANK], wg_raw,
                                          gate_w[:, :, 0:RANK].bitcast(F32), ALU.subtract).then_inc(wg_lo, 1)
                    if c == 5:
                        dve.wait_ge(par_turned, 2)
                        dve.tensor_copy(par[:, KT:P], aux[:, 1, KT:P]).then_inc(par_ready, 1)
                    if c == 7:
                        dve.wait_ge(low_ready, 1)
                        dve.tensor_copy(g_low, aux[:, 0, 0:S]).then_inc(low_out, 1)
                        dve.wait_ge(sq_ready, 2)
                        mean(ST_X, sums[:, Q_X:Q_X + 2], D)
                if t == 1 and c == 0:
                    dve.wait_ge(rs_ready, 1)
                    dve.tensor_scalar(scl[:, R1S:R1S + 2], rs[:, ST_X, 0:2], GDK ** -0.5, None, ALU.mult)
                    link(dve.tensor_scalar(scl[:, R1H:R1H + 2], rs[:, ST_X, 0:2], 0.5, None, ALU.mult))
                    dve.sem_inc(r1_ready, 1)
                if t == 1:
                    if c in (1, 2):
                        for i in (2 * c - 2, 2 * c - 1):
                            tt, half = divmod(i, 2)
                            dve.wait_ge(gate_ready, i + 1)
                            dve.scalar_tensor_tensor(
                                out=z_gate[:, i, :], in0=aux[:, (i + 1) % 2, :],
                                scalar=rs[:, ST_X, tt:tt + 1], in1=b_gate[:, half * N:(half + 1) * N],
                                op0=ALU.mult, op1=ALU.add).then_inc(gate_out, 1)
                    if c in (4, 6):
                        tt = (c - 4) // 2
                        dve.wait_ge(ln_ready, tt + 1)
                        dve.wait_ge(gate_out, 4)
                        dve.scalar_tensor_tensor(
                            out=log_a[:, tt, :],
                            in0=z_gate[:, 2 * tt:2 * tt + 2, :].rearrange("p a b -> p (a b)"),
                            scalar=0.0, in1=log_a[:, tt, :], op0=ALU.min, op1=ALU.subtract)\
                            .then_inc(log_ready, 1)
                if t == 2:
                    if c == 1:
                        dve.wait_ge(lam_act, 1)
                        lam = par[:, C_LAM:C_LAM + 8]
                        link(dve.tensor_scalar(lru_par[:, L_SP:L_SP + 8], lam, -1.0, 0.0, ALU.mult, ALU.max))
                        link(dve.tensor_tensor(lru_par[:, L_SP:L_SP + 8], lru_par[:, L_SP:L_SP + 8],
                                               lru_par[:, L_T:L_T + 8], ALU.add))
                        link(dve.tensor_scalar(lru_par[:, L_SP:L_SP + 8], lru_par[:, L_SP:L_SP + 8],
                                               LRU_C / 2, None, ALU.mult))
                        link(dve.tensor_scalar(lru_par[:, L_NEG:L_NEG + 8], lru_par[:, L_SP:L_SP + 8],
                                               -1.0, None, ALU.mult))
                        dve.wait_ge(gain_in, 48)
                        link(dve.tensor_scalar(lru_par[:, L_BA:L_BA + 16], par[:, C_BA:C_BA + 16], 0.5,
                                               None, ALU.mult))
                        dve.scalar_tensor_tensor(out=qk_gain[:, 2:3], in0=qk_gain[:, 0:1],
                                                 scalar=HD ** -0.5, in1=qk_gain[:, 1:2],
                                                 op0=ALU.mult, op1=ALU.mult).then_inc(lam_ready, 1)
                    if c in (2, 4):
                        tt = c // 2 - 1
                        dve.wait_ge(suf_out, c)
                        dve.wait_ge(acc_read_act, 2)
                        dve.tensor_tensor(keys[:, tt, :], keys[:, tt, :], log_a[:, tt, :], ALU.mult)\
                            .then_inc(keys_ready, 1)
                    if c == 6:
                        move_second(key_t[:, 2:4, :], groups_before(2) + 2)
                if t == 3 and c == 1:
                    move_second(key_t[:, 6:8, :], groups_before(2) + 4)
                    for a in (0, S):
                        dve.memset(scores[64:128, :, a:a + 64], 0.0)
                if (t, c) in DECAYS:
                    decay_head(DECAYS.index((t, c)))
                if (t, c) in SCORES_OUT:
                    hd = SCORES_OUT.index((t, c))
                    dve.wait_ge(sc_ready, hd + 1)
                    dve.tensor_copy(scores[64:128, hd, 64:S], aux[64:128, hd % 2, 64:S])
                    dve.tensor_copy(scores[64:128, hd, S + 64:S + P], aux[64:128, hd % 2, 2 * S - 64:2 * S])\
                        .then_inc(sc_dve, 1)
                if prev == "v" and c == 4:
                    hd = (t - 1 - FIRST_V) // 2
                    dve.wait_ge(sq_ready, 2 + 2 * hd + 2)
                    mean(ST_O + hd, sums[:, Q_O + 2 * hd:Q_O + 2 * hd + 2], N)
                for j in range(2):
                    taps = CONV_TAPS[j].get(CH * (t - FIRST_X - 1 - j) + c, ())
                    if 3 in taps:
                        dve.wait_ge(tp_hi, groups_before(t + 1))
                        dve.wait_ge(tp_lo, groups_before(t + 1))
                        if j == 1:
                            dve.wait_ge(lru_mm, 4)
                    for w in taps:
                        for i in range(4):
                            col = C_CONV + 8 * w + 4 * j + i
                            wcol = par[:, col:col + 1]
                            if w == 3:
                                ins = dve.tensor_scalar(
                                    conv[:, i, :], lru_x[:, i, w:w + S], wcol,
                                    par[:, C_CB + 4 * j + i:C_CB + 4 * j + i + 1], ALU.mult, ALU.add)
                            else:
                                ins = dve.scalar_tensor_tensor(
                                    out=conv[:, i, :], in0=lru_x[:, i, w:w + S], scalar=wcol,
                                    in1=conv[:, i, :], op0=ALU.mult, op1=ALU.add)
                        if w:
                            link(ins)
                        else:
                            ins.then_inc(conv_ready, 1)
                for j in range(2):
                    step = lru_step(t, c, j)
                    if step == 3:
                        dve.wait_ge(lru_th, 4 * j + 4)
                        link(dve.scalar_tensor_tensor(out=th_i, in0=th_i, scalar=1.0, in1=conv,
                                                      op0=ALU.add, op1=ALU.mult))
                    if step == 4:
                        dve.wait_ge(lru_exp, j + 1)
                        link(dve.tensor_tensor(th_r, lru_a, lru_a, ALU.mult))
                        dve.scalar_tensor_tensor(out=lru_u, in0=th_r, scalar=1.0, in1=lru_u,
                                                 op0=ALU.add, op1=ALU.mult).then_inc(lru_sq, 1)
                    if step == 7:
                        dve.wait_ge(lru_root, j + 1)
                        link(dve.tensor_tensor(th_i, lru_u, th_i, ALU.mult))
                        for i in range(4):
                            ins = dve.tensor_tensor_scan(lru_h[:, 4 * j + i, :], lru_a[:, i, :],
                                                         th_i[:, i, :], 0.0, ALU.mult, ALU.add)
                        ins.then_inc(lru_done, 1)
                if prev and prev in "KQ":
                    i = q - FIRST_K2
                    if c == 2:
                        dve.wait_ge(kq_red, i + 1)
                        s8 = sums[:, Q_KQ + 8 * i:Q_KQ + 8 * i + 8]
                        link(dve.tensor_reduce(s8.rearrange("p (t n) -> p t n", n=4),
                                               sq2.rearrange("p t (n d) -> p t n d", d=HD), AX.X, ALU.add))
                        mean(ST_KQ + i, s8, HD)
                    if c == 3:
                        dve.wait_ge(rs_ready, ST_KQ + i + 1)
                        st = stage[:, b, :, :].rearrange("p t (n d) -> p (t n) d", d=HD)
                        dve.tensor_tensor(st, st, rs[:, ST_KQ + i, :].unsqueeze(2).to_broadcast([P, 8, HD]),
                                          ALU.mult).then_inc(stage_dve, 1)
                if ATTEND <= t < ATTEND_END:
                    if c in (1, 2):
                        hd = 2 * (t - ATTEND) + c - 1
                        dve.wait_ge(ln_out, hd + 1)
                        i = hd % 2
                        link(dve.scalar_tensor_tensor(out=soft_sp[:, i, :], in0=aux[:, i, 0:384],
                                                      scalar=0.0, in1=soft[:, i, :], op0=ALU.max,
                                                      op1=ALU.add))
                        link(dve.tensor_copy(sp_hi[:, i, :], soft_sp[:, i, :]))
                        dve.tensor_tensor(sp_lo[:, i, :], soft_sp[:, i, :], sp_hi[:, i, :].bitcast(F32),
                                          ALU.subtract).then_inc(sp_out, 1)
                    if c in (5, 6):
                        hd = 2 * (t - ATTEND) + c - 5
                        dve.wait_ge(y_ready, hd + 1)
                        dve.tensor_copy(y_t[:, hd, :], aux[:, hd % 2, 0:S]).then_inc(y_out, 1)

            def run(t, it=None):
                for c in range(CH):
                    before(t, c, it)
                    if t < PANELS:
                        split_lo(t, c, it)

            dve.wait_ge(par_turned, 1)
            dve.tensor_copy(par[:, 0:KT], aux[:, 1, 0:KT]).then_inc(par_ready, 1)
            dve.wait_ge(par_ready, 1)
            for n in range(RING):
                if n:
                    rest_x(n % 2, xa_hi, xa_lo, 2 * n, C_GLA, n + 1)
                dve.wait_ge(hi_ready, n + 1)
                dve.tensor_tensor(w_lo[:, n, :, :], raw[:, n, :, :], w_hi[:, n, :, :].bitcast(F32),
                                  ALU.subtract).then_inc(lo_ready, 1)
                if n == 0:
                    rest_x(0, xa_hi, xa_lo, 0, C_GLA, 1)
            for t in range(FIRST_U + 1):
                run(t)
            with dve.Fori(0, MLP_BLOCKS - 1) as it:
                for t in range(FIRST_U + 1, FIRST_U + 1 + BODY):
                    run(t, it)
            for t in range(FIRST_U + 1 + BODY * (MLP_BLOCKS - 1), PANELS + 1):
                run(t)


_INS = ["x", "gla_norm", "gla_w_in", "gla_w_gate_up", "gla_b_gate", "gla_o_norm", "gla_w_out",
        "mlp_norm", "mlp_w_up", "mlp_w_down", "final_norm", "norm_gain_2", "w_in_2",
        "q_norm_gain_2", "k_norm_gain_2", "conv_w_2", "conv_b_2", "lru_w_a_2", "lru_b_a_2",
        "lru_w_x_2", "lru_b_x_2", "lru_lambda_2", "w_out_2"]
_OUT = (1, S, D)


def kernel(**inputs):
    import numpy as np
    import concourse.bacc as bacc
    from concourse.bass_utils import run_bass_kernel_spmd as run

    nc = bacc.Bacc("TRN2", target_bir_lowering=False, num_devices=1)
    arrays, args = {}, []
    for name in _INS:
        a = np.ascontiguousarray(inputs[name])
        arrays[f"in_{name}"] = a
        args.append(nc.dram_tensor(f"in_{name}", a.shape, F32, kind="ExternalInput").ap())
    out = nc.dram_tensor("result", _OUT, F32, kind="ExternalOutput").ap()
    gated_block_kernel(nc, *args, out)
    return run(nc, [arrays], core_ids=[0]).results[0]["result"]
```
